# Optimizing a Trainium2 kernel written in Bass

```python
import jax, jax.numpy as jnp
from jax import lax
import numpy as np

D_MODEL = 1024
BATCH = 1
SEQ = 1024
DEPTH = 2

GRID_W = 64
CTX_LEN = 256
N_EVEN = (DEPTH + 1) // 2
N_ODD = DEPTH // 2
RET_HEADS = 4
RET_DK = 128
RET_DV = 128
RET_CHUNK = 128
CONV_CH = D_MODEL // 2
CONV_WIDTH = 31
MLA_HEADS = 8
MLA_Q_LORA = D_MODEL // 2
MLA_KV_LORA = D_MODEL // 4
MLA_NOPE = 128
MLA_ROPE = 64
MLA_V = 128
MLA_QK = MLA_NOPE + MLA_ROPE
ATTN_BLOCK = 128
N_EXPERTS = 16
EC_CAPACITY_FACTOR = 2
EXPERT_FF = 1024
ROPE_BASE = 10000.0
EPS = 1e-6

A_QK = RET_HEADS * RET_DK
A_V = RET_HEADS * RET_DV
EVEN_SPLIT = (A_QK, 2 * A_QK, 2 * A_QK + A_V, 2 * A_QK + 2 * A_V, 2 * A_QK + 3 * A_V, 2 * A_QK + 3 * A_V + CONV_CH)
EVEN_IN = 2 * A_QK + 3 * A_V + 2 * CONV_CH
EVEN_MIX = A_V + CONV_CH
ODD_SPLIT = (MLA_Q_LORA, MLA_Q_LORA + MLA_KV_LORA)
ODD_IN = MLA_Q_LORA + MLA_KV_LORA + MLA_ROPE
ODD_MIX = MLA_HEADS * MLA_V

kernel_name = "hybrid_retention_conv_mla_ecmoe_dit"

def rms_norm(x, g):
    xf = x.astype(jnp.float32)
    y = xf * lax.rsqrt(jnp.mean(xf * xf, axis=-1, keepdims=True) + EPS)
    return (y * g.astype(jnp.float32)).astype(x.dtype)

def ada_modulate(x, g, shift, scale):
    return rms_norm(x, g) * (1 + scale) + shift

def grid_positions(n):
    n_rows = n // GRID_W
    row = jnp.repeat(jnp.arange(n_rows, dtype=jnp.float32), GRID_W)
    col = jnp.tile(jnp.arange(GRID_W, dtype=jnp.float32), n_rows)
    return row, col

def axial_rope(x, row, col):
    half = x.shape[-1] // 2
    nf = half // 2
    inv = ROPE_BASE ** (-(jnp.arange(nf, dtype=jnp.float32) / nf))
    xf = x.astype(jnp.float32)

    def rot(seg, pos):
        ang = pos[:, None] * inv[None, :]
        cos, sin = jnp.cos(ang), jnp.sin(ang)
        s1, s2 = seg[..., :nf], seg[..., nf:]
        return jnp.concatenate([s1 * cos - s2 * sin, s2 * cos + s1 * sin], axis=-1)

    return jnp.concatenate([rot(xf[..., :half], row), rot(xf[..., half:], col)], axis=-1).astype(x.dtype)

def to_heads(p, n_heads):
    b, n, _ = p.shape
    return p.reshape(b, n, n_heads, -1).transpose(0, 2, 1, 3)

def from_heads(o):
    b, h, n, d = o.shape
    return o.transpose(0, 2, 1, 3).reshape(b, n, h * d)

def flip_seq(t):
    return jnp.flip(t, axis=2)

def retention_chunkwise(q, k, v, log_gamma, state0):
    b, h, n, _ = q.shape
    dv = v.shape[-1]
    L = RET_CHUNK
    nc = n // L

    def chunks(t):
        return t.reshape(b, h, nc, L, t.shape[-1]).transpose(2, 0, 1, 3, 4)

    pos = jnp.arange(L, dtype=jnp.float32)
    lg = log_gamma.astype(jnp.float32)
    diff = pos[:, None] - pos[None, :]
    intra = jnp.where(diff >= 0, jnp.exp(lg[:, None, None] * jnp.maximum(diff, 0.0)), 0.0)
    xi = jnp.exp(lg[:, None] * (pos + 1.0))[:, :, None]
    zeta = jnp.exp(lg[:, None] * (L - 1.0 - pos))[:, :, None]
    decay_chunk = jnp.exp(lg * L)[:, None, None]

    def step(state, qkv):
        qc, kc, vc = qkv
        s = jnp.einsum('bhid,bhjd->bhij', qc, kc) * intra
        o = jnp.einsum('bhij,bhjv->bhiv', s, vc) + jnp.einsum('bhid,bhdv->bhiv', qc, state) * xi
        state = state * decay_chunk + jnp.einsum('bhjd,bhjv->bhdv', kc * zeta, vc)
        return state, o

    state, o = lax.scan(step, state0.astype(jnp.float32), (chunks(q), chunks(k), chunks(v)))
    return o.transpose(1, 2, 0, 3, 4).reshape(b, h, n, dv), state

def head_group_norm(o, g):
    mu = jnp.mean(o, axis=-1, keepdims=True)
    var = jnp.mean(jnp.square(o - mu), axis=-1, keepdims=True)
    return from_heads((o - mu) * lax.rsqrt(var + EPS)) * g.astype(jnp.float32)

def conformer_conv(bv, bg, conv_w, conv_b, ln_g, ln_b):
    u = bv * jax.nn.sigmoid(bg)
    y = lax.conv_general_dilated(
        u, conv_w[:, None, :].astype(u.dtype), window_strides=(1,),
        padding=[(CONV_WIDTH // 2, CONV_WIDTH // 2)],
        dimension_numbers=('NWC', 'WIO', 'NWC'), feature_group_count=CONV_CH) + conv_b
    yf = y.astype(jnp.float32)
    mu = jnp.mean(yf, axis=-1, keepdims=True)
    var = jnp.mean(jnp.square(yf - mu), axis=-1, keepdims=True)
    yn = (yf - mu) * lax.rsqrt(var + EPS) * ln_g.astype(jnp.float32) + ln_b.astype(jnp.float32)
    return jax.nn.silu(yn).astype(bv.dtype)

def even_mixer(hx, hc, w_in, logit_f, logit_b, gn_g, conv_w, conv_b, ln_g, ln_b, w_out, row, col, need_ctx):
    f32 = jnp.float32
    lg_f = jax.nn.log_sigmoid(logit_f.astype(f32))
    lg_b = jax.nn.log_sigmoid(logit_b.astype(f32))

    def branch(h, rope):
        q, k, v, gf, gb, bv, bg = jnp.split(h @ w_in, EVEN_SPLIT, axis=-1)
        q = to_heads(q, RET_HEADS).astype(f32)
        k = to_heads(k, RET_HEADS).astype(f32) * (RET_DK ** -0.5)
        v = to_heads(v, RET_HEADS).astype(f32)
        if rope:
            q = axial_rope(q, row, col)
            k = axial_rope(k, row, col)
        return q, k, v, gf, gb, bv, bg

    def merge(o_f, o_b, gf, gb, bv, bg, dtype):
        ret = head_group_norm(o_f, gn_g) * jax.nn.silu(gf.astype(f32)) \
            + head_group_norm(o_b, gn_g) * jax.nn.silu(gb.astype(f32))
        conv = conformer_conv(bv, bg, conv_w, conv_b, ln_g, ln_b)
        return jnp.concatenate([ret.astype(dtype), conv.astype(dtype)], axis=-1) @ w_out

    qc, kc, vc, gfc, gbc, bvc, bgc = branch(hc, False)
    b = hc.shape[0]
    zero = jnp.zeros((b, RET_HEADS, RET_DK, RET_DV), f32)
    oc_f, st_f = retention_chunkwise(qc, kc, vc, lg_f, zero)
    oc_b, st_b = retention_chunkwise(flip_seq(qc), flip_seq(kc), flip_seq(vc), lg_b, zero)
    qx, kx, vx, gfx, gbx, bvx, bgx = branch(hx, True)
    ox_f, _ = retention_chunkwise(qx, kx, vx, lg_f, st_f)
    ox_b, _ = retention_chunkwise(flip_seq(qx), flip_seq(kx), flip_seq(vx), lg_b, st_b)

    out_x = merge(ox_f, flip_seq(ox_b), gfx, gbx, bvx, bgx, hx.dtype)
    out_c = merge(oc_f, flip_seq(oc_b), gfc, gbc, bvc, bgc, hc.dtype) if need_ctx else None
    return out_x, out_c

def mla_project(h, w_in, q_a_g, kv_a_g, w_uq, w_ukv, qk_g_q, qk_g_k, pos):
    b, n, _ = h.shape
    c_q, c_kv, k_pe = jnp.split(h @ w_in, ODD_SPLIT, axis=-1)
    q = to_heads(rms_norm(c_q, q_a_g) @ w_uq, MLA_HEADS)
    kv = to_heads(rms_norm(c_kv, kv_a_g) @ w_ukv, MLA_HEADS)
    k_nope, v = kv[..., :MLA_NOPE], kv[..., MLA_NOPE:]
    k_pe = jnp.broadcast_to(k_pe[:, None], (b, MLA_HEADS, n, MLA_ROPE))
    k = jnp.concatenate([k_nope, k_pe], axis=-1)
    q = rms_norm(q, qk_g_q)
    k = rms_norm(k, qk_g_k)
    if pos is not None:
        row, col = pos
        q = jnp.concatenate([q[..., :MLA_NOPE], axial_rope(q[..., MLA_NOPE:], row, col)], axis=-1)
        k = jnp.concatenate([k[..., :MLA_NOPE], axial_rope(k[..., MLA_NOPE:], row, col)], axis=-1)
    return q, k, v

def blocked_attention(q, k, v):
    b, h, n, d = q.shape
    nb = n // ATTN_BLOCK
    scale = d ** -0.5
    qb = q.reshape(b, h, nb, ATTN_BLOCK, d).transpose(2, 0, 1, 3, 4)

    def one(qblk):
        s = jnp.einsum('bhqd,bhkd->bhqk', qblk, k).astype(jnp.float32) * scale
        p = jax.nn.softmax(s, axis=-1)
        return jnp.einsum('bhqk,bhkd->bhqd', p.astype(v.dtype), v)

    o = lax.map(one, qb)
    return o.transpose(1, 2, 0, 3, 4).reshape(b, h, n, v.shape[-1])

def odd_mixer(hx, hc, w_in, q_a_g, kv_a_g, w_uq, w_ukv, qk_g_q, qk_g_k, w_out, row, col, need_ctx):
    qx, kx, vx = mla_project(hx, w_in, q_a_g, kv_a_g, w_uq, w_ukv, qk_g_q, qk_g_k, (row, col))
    qc, kc, vc = mla_project(hc, w_in, q_a_g, kv_a_g, w_uq, w_ukv, qk_g_q, qk_g_k, None)
    ox = blocked_attention(qx, jnp.concatenate([kx, kc], axis=2), jnp.concatenate([vx, vc], axis=2))
    out_x = from_heads(ox) @ w_out
    out_c = from_heads(blocked_attention(qc, kc, vc)) @ w_out if need_ctx else None
    return out_x, out_c

def ec_moe(h, router_w, w_gate, w_up, w_down):
    b, n, d = h.shape
    cap = max(1, (EC_CAPACITY_FACTOR * n) // N_EXPERTS)
    aff = jax.nn.softmax(jnp.einsum('bnd,de->bne', h, router_w).astype(jnp.float32), axis=-1)
    gates, idx = lax.top_k(aff.transpose(0, 2, 1), cap)
    xs = jax.vmap(lambda hb, ib: hb[ib])(h, idx)
    a = jnp.einsum('becd,edf->becf', xs, w_gate)
    u = jnp.einsum('becd,edf->becf', xs, w_up)
    y = jnp.einsum('becf,efd->becd', jax.nn.silu(a) * u, w_down) * gates[..., None].astype(h.dtype)
    return jax.vmap(lambda yb, ib: jnp.zeros((n, d), h.dtype).at[ib.reshape(-1)].add(yb.reshape(-1, d)))(y, idx)

def setup_inputs(seed: int = 0) -> dict:
    key = jax.random.key(seed)
    ks = jax.random.split(key, 32)
    f32 = jnp.float32

    def nrm(k, shape, scale):
        return jax.random.normal(k, shape, f32) * scale

    def gain(k, shape):
        return 1.0 + 0.02 * jax.random.normal(k, shape, f32)

    decay_logit = jnp.asarray(np.log(2.0 ** (5.0 + np.arange(RET_HEADS)) - 1.0).astype(np.float32))
    return {
        "x": nrm(ks[0], (BATCH, SEQ, D_MODEL), 1.0),
        "c": nrm(ks[1], (BATCH, D_MODEL), 1.0),
        "ctx": nrm(ks[2], (BATCH, CTX_LEN, D_MODEL), 1.0),
        "c_ctx": nrm(ks[3], (D_MODEL,), 1.0),
        "mod_w": nrm(ks[4], (DEPTH, D_MODEL, 6 * D_MODEL), 0.5 * D_MODEL ** -0.5),
        "mod_b": nrm(ks[5], (DEPTH, 6 * D_MODEL), 0.01),
        "norm1_g": gain(ks[6], (DEPTH, D_MODEL)),
        "norm2_g": gain(ks[7], (DEPTH, D_MODEL)),
        "ev_w_in": nrm(ks[8], (N_EVEN, D_MODEL, EVEN_IN), D_MODEL ** -0.5),
        "ret_decay_f": decay_logit[None] + nrm(ks[9], (N_EVEN, RET_HEADS), 0.01),
        "ret_decay_b": decay_logit[None] + nrm(ks[10], (N_EVEN, RET_HEADS), 0.01),
        "ret_gn_g": gain(ks[11], (N_EVEN, A_V)),
        "conv_w": nrm(ks[12], (N_EVEN, CONV_WIDTH, CONV_CH), CONV_WIDTH ** -0.5),
        "conv_b": nrm(ks[13], (N_EVEN, CONV_CH), 0.01),
        "conv_ln_g": gain(ks[14], (N_EVEN, CONV_CH)),
        "conv_ln_b": nrm(ks[15], (N_EVEN, CONV_CH), 0.01),
        "ev_w_out": nrm(ks[16], (N_EVEN, EVEN_MIX, D_MODEL), EVEN_MIX ** -0.5),
        "od_w_in": nrm(ks[17], (N_ODD, D_MODEL, ODD_IN), D_MODEL ** -0.5),
        "mla_q_a_g": gain(ks[18], (N_ODD, MLA_Q_LORA)),
        "mla_kv_a_g": gain(ks[19], (N_ODD, MLA_KV_LORA)),
        "mla_w_uq": nrm(ks[20], (N_ODD, MLA_Q_LORA, MLA_HEADS * MLA_QK), MLA_Q_LORA ** -0.5),
        "mla_w_ukv": nrm(ks[21], (N_ODD, MLA_KV_LORA, MLA_HEADS * (MLA_NOPE + MLA_V)), MLA_KV_LORA ** -0.5),
        "mla_qk_g_q": gain(ks[22], (N_ODD, MLA_QK)),
        "mla_qk_g_k": gain(ks[23], (N_ODD, MLA_QK)),
        "od_w_out": nrm(ks[24], (N_ODD, ODD_MIX, D_MODEL), ODD_MIX ** -0.5),
        "router_w": nrm(ks[25], (DEPTH, D_MODEL, N_EXPERTS), D_MODEL ** -0.5),
        "moe_w_gate": nrm(ks[26], (DEPTH, N_EXPERTS, D_MODEL, EXPERT_FF), D_MODEL ** -0.5),
        "moe_w_up": nrm(ks[27], (DEPTH, N_EXPERTS, D_MODEL, EXPERT_FF), D_MODEL ** -0.5),
        "moe_w_down": nrm(ks[28], (DEPTH, N_EXPERTS, EXPERT_FF, D_MODEL), EXPERT_FF ** -0.5),
    }

def reference(x, c, ctx, c_ctx, mod_w, mod_b, norm1_g, norm2_g, ev_w_in, ret_decay_f, ret_decay_b,
              ret_gn_g, conv_w, conv_b, conv_ln_g, conv_ln_b, ev_w_out, od_w_in, mla_q_a_g, mla_kv_a_g,
              mla_w_uq, mla_w_ukv, mla_qk_g_q, mla_qk_g_k, od_w_out, router_w, moe_w_gate, moe_w_up,
              moe_w_down):
    row, col = grid_positions(x.shape[1])
    silu_c = jax.nn.silu(c)
    silu_cc = jax.nn.silu(c_ctx)
    for l in range(DEPTH):
        need_ctx = l < DEPTH - 1
        mod_x = (silu_c @ mod_w[l] + mod_b[l])[:, None, :]
        mod_c = silu_cc @ mod_w[l] + mod_b[l]
        sh1, sc1, g1, sh2, sc2, g2 = jnp.split(mod_x, 6, axis=-1)
        sh1c, sc1c, g1c, sh2c, sc2c, g2c = jnp.split(mod_c, 6, axis=-1)
        hx = ada_modulate(x, norm1_g[l], sh1, sc1)
        hc = ada_modulate(ctx, norm1_g[l], sh1c, sc1c)
        i = l // 2
        if l % 2 == 0:
            ox, oc = even_mixer(hx, hc, ev_w_in[i], ret_decay_f[i], ret_decay_b[i], ret_gn_g[i], conv_w[i],
                                conv_b[i], conv_ln_g[i], conv_ln_b[i], ev_w_out[i], row, col, need_ctx)
        else:
            ox, oc = odd_mixer(hx, hc, od_w_in[i], mla_q_a_g[i], mla_kv_a_g[i], mla_w_uq[i], mla_w_ukv[i],
                               mla_qk_g_q[i], mla_qk_g_k[i], od_w_out[i], row, col, need_ctx)
        x = x + g1 * ox
        hx = ada_modulate(x, norm2_g[l], sh2, sc2)
        x = x + g2 * ec_moe(hx, router_w[l], moe_w_gate[l], moe_w_up[l], moe_w_down[l])
        if need_ctx:
            ctx = ctx + g1c * oc
            hc = ada_modulate(ctx, norm2_g[l], sh2c, sc2c)
            ctx = ctx + g2c * ec_moe(hc, router_w[l], moe_w_gate[l], moe_w_up[l], moe_w_down[l])
    return x


_drawn_inputs = setup_inputs


def setup_inputs(seed=0):
    import zlib

    import numpy as np

    out = dict(_drawn_inputs(seed))
    spreads = {}
    factors = {'mod_b': 4.068,
     'norm1_g': 5.51,
     'norm2_g': 6.19,
     'ret_gn_g': 8.0,
     'conv_b': 23.862,
     'conv_ln_g': 28.263,
     'conv_ln_b': 44.456,
     'mla_q_a_g': 8.0,
     'mla_kv_a_g': 8.0,
     'mla_w_uq': 2.741,
     'mla_qk_g_q': 8.0,
     'mla_qk_g_k': 8.0}
    for name, (base, spread) in spreads.items():
        noise = np.random.default_rng([zlib.crc32(name.encode()), seed]).standard_normal(out[name].shape)
        drawn = base * np.exp(spread * noise) if base else spread * noise
        out[name] = __import__('jax').numpy.asarray(drawn.astype(out[name].dtype))
    for name, factor in factors.items():
        out[name] = (out[name] * factor).astype(out[name].dtype)
    return out
```

```python
from contextlib import ExitStack

import concourse.bass as bass
from concourse import mybir

F32 = mybir.dt.float32
F32R = mybir.dt.float32r
U32 = mybir.dt.uint32
ALU = mybir.AluOpType
ACT = mybir.ActivationFunctionType
AX = mybir.AxisListType

P = 128
D = 1024
KD = D // P
SEQ = 1024
CTX = 256
XT = SEQ // P
CT = CTX // P
NT = XT + CT
TOK = SEQ + CTX
HALF = D // 2
BANK = 512
DEPTH = 2
EPS = 1e-6
NMOD = 6 * D
SH1, SC1, G1, SH2, SC2, G2 = range(6)

HEADS = 4
HD = 128
TAPS = 31
PADT = TAPS // 2
UX0 = PADT
UC0 = SEQ + 2 * PADT + PADT
UW = TOK + 4 * PADT
EVC = 7
C_BV, C_BG, C_Q, C_K, C_V, C_GF, C_GB = range(EVC)
R_QT, R_KT, R_K, R_V, R_GF, R_GB = range(6)
RECW = 6 * HALF

AH = 8
NOPE = 128
ROPE = 64
QKD = NOPE + ROPE
QL = 512
KVL = 256
KEYT = NT

NE = 16
FF = 1024
FB = FF // P
CAPX = 2 * SEQ // NE
CAPC = 2 * CTX // NE
PIECES = 12
PREFETCH = (PIECES // 2, PIECES)
PW = KD * 256
WOUT = KD * D


class Signals:

    def __init__(self, nc, stage):
        self.nc, self.stage, self.held = nc, stage, []

    def __call__(self, name):
        s = self.nc.alloc_semaphore(self.stage + "_" + name)
        self.held.append(s)
        return s

    def pair(self, name):
        return [self(name + "0"), self(name + "1")]

    def release(self):
        self.nc.clear_and_free_semaphores(self.held)
        self.nc.all_engine_barrier()


def tiles_of(nc, st, stage):
    def tile(name, shape, dt=F32):
        return st.enter_context(nc.sbuf_tensor(stage + "_" + name, shape, dt))
    return tile


class Carve:

    def __init__(self, ring, at):
        self.ring, self.at = ring, at

    def __call__(self, width):
        piece = self.ring[:, self.at:self.at + width]
        self.at += width
        assert self.at <= EVC * 2 * PW
        return piece


def rows(dram, t, n=P):
    return dram[bass.ds(t * P, n), :]


def settle(eng, g):
    eng.sem_inc(g.tick, 1)


def mod_row(mod_d, stream, layer, which):
    a = layer * NMOD + which * D
    return mod_d[stream, a:a + D].partition_broadcast(P)


class Modulation:
    DEEP = 4
    ITER = NMOD // BANK // DEEP

    def __init__(self, nc, io, g, tile, sem, layer):
        self.nc, self.io, self.g, self.layer = nc, io, g, layer
        self.w = [tile(f"w{u}", [P, KD, BANK]) for u in range(self.DEEP)]
        self.bias = [tile(f"bias{u}", [1, BANK]) for u in range(self.DEEP)]
        self.row = [tile(f"row{u}", [2, BANK]) for u in range(self.DEEP)]
        self.cc, self.sc, self.ones = tile("cc", [P, KD * 2]), tile("sc", [P, KD * 2]), tile("ones", [1, 2])
        self.c_in, self.c_silu, self.ones_set = sem("c_in"), sem("c_silu"), sem("ones_set")
        self.w_in = [sem(f"w_in{u}") for u in range(self.DEEP)]
        self.summed = sem("summed")
        self.bank_free = sem("bank_free")
        self.row_out = [sem(f"row_out{u}") for u in range(self.DEEP)]

    def sync(self, sp):
        sp.dma_start(self.cc[:, :], self.io["cc"]).then_inc(self.c_in, 16)
        first = self.layer * NMOD // BANK
        with sp.Fori(0, self.ITER) as i:
            for u in range(self.DEEP):
                sp.wait_ge(self.summed, self.DEEP * i + u + 1)
                settle(sp, self.g)
                sp.dma_start(self.w[u][:, :, :].rearrange("p k n -> p (k n)"),
                             rows(self.io["mod_w"], self.DEEP * i + (u + first))).then_inc(self.w_in[u], 16)
                sp.dma_start(self.bias[u][:, :], self.io["mod_b"][bass.ds(self.DEEP * i + (u + first), 1), :]).then_inc(
                    self.w_in[u], 16)

    def vector(self):
        self.nc.vector.memset(self.ones[:, :], 1.0).then_inc(self.ones_set, 1)

    def scalar(self, act):
        act.sem_inc(self.bank_free, self.DEEP)
        for u in range(self.DEEP):
            act.sem_inc(self.row_out[u], 16)
        act.wait_ge(self.c_in, 16)
        self.nc.scalar.activation(self.sc[:, :], self.cc[:, :], ACT.Silu).then_inc(self.c_silu, 1)
        with act.Fori(0, self.ITER) as i:
            for u in range(self.DEEP):
                act.wait_ge(self.summed, self.DEEP * i + u + 1 + self.DEEP)
                act.wait_ge(self.row_out[u], 16 * (i + 1))
                self.nc.scalar.copy(self.row[u][:, :], self.g.psum[0:2, 4 + u, :]).then_inc(self.bank_free, 1)
                act.wait_ge(self.bank_free, self.DEEP * i + u + 1 + self.DEEP)
                col = (self.DEEP * i + u) * BANK + self.layer * NMOD
                act.dma_start(self.io["mod_d"][:, bass.ds(col, BANK)], self.row[u][:, :]).then_inc(self.row_out[u], 16)
        for u in range(self.DEEP):
            act.wait_ge(self.row_out[u], 16 * (self.ITER + 1))

    def tensor(self, pe):
        pe.sem_inc(self.summed, self.DEEP)
        pe.wait_ge(self.c_silu, 1)
        pe.wait_ge(self.ones_set, 1)
        with pe.Fori(0, self.ITER) as i:
            for u in range(self.DEEP):
                pe.wait_ge(self.w_in[u], 32 * (i + 1))
                pe.wait_ge(self.bank_free, self.DEEP * i + u + 1)
                for k in range(KD):
                    self.nc.tensor.matmul(self.g.psum[0:2, 4 + u, :], self.sc[:, 2 * k:2 * k + 2], self.w[u][:, k, :],
                                          start=(k == 0), stop=False)
                self.nc.tensor.matmul(self.g.psum[0:2, 4 + u, :], self.ones[:, :], self.bias[u][:, :],
                                      start=False, stop=True).then_inc(self.summed, 1)


def modulation(nc, io, g):
    with ExitStack() as st:
        sem = Signals(nc, "mod")
        mod = Modulation(nc, io, g, tiles_of(nc, st, "mod"), sem, 0)
        with nc.Block() as block:
            @block.sync
            def _(sp):
                sp.dma_start(g.ident[:, :], io["ident_d"]).then_inc(g.ident_in, 16)
                mod.sync(sp)
                for c in range(C_Q):
                    sp.dma_start(g.ring[:, c * 2 * PW:(c + 1) * 2 * PW], rows(io["ev_w_in"], c)).then_inc(g.ev_conv_in, 16)

            @block.vector
            def _(dve):
                mod.vector()

            @block.gpsimd
            def _(pool):
                nc.gpsimd.memset(g.mhalf[:, :], -0.5).then_inc(g.mhalf_set, 1)

            @block.scalar
            def _(act):
                mod.scalar(act)

            @block.tensor
            def _(pe):
                mod.tensor(pe)
        sem.release()


class At:

    def __init__(self, i, b):
        self.i, self.b, self.t = i, b, 2 * i + b

    def plus(self, n):
        return At(self.i + (self.b + n) // 2, (self.b + n) % 2)

    def exists(self, n):
        return not isinstance(self.i, int) or 0 <= self.t < n

    def stream(self):
        return int(isinstance(self.i, int) and self.t >= XT)


def run(eng, step, pairs, lo, hi):
    for i in range(lo):
        step(At(i, 0))
        step(At(i, 1))
    if hi > lo:
        with eng.Fori(lo, hi) as i:
            step(At(i, 0))
            step(At(i, 1))
    for i in range(max(lo, hi), pairs):
        step(At(i, 0))
        step(At(i, 1))


class Norm:

    def __init__(self, nc, g, tile, sem):
        self.nc, self.g = nc, g
        self.arow = [tile(f"arow{s}", [P, D]) for s in range(2)]
        self.brow = [tile(f"brow{s}", [P, D]) for s in range(2)]
        self.sq = tile("sq", [P, D])
        self.x = [tile(f"x{b}", [P, D]) for b in range(2)]
        self.h = [tile(f"h{b}", [P, D]) for b in range(2)]
        self.ssq = [tile(f"ssq{b}", [P, 1]) for b in range(2)]
        self.ms = [tile(f"ms{b}", [P, 1]) for b in range(2)]
        self.rstd = [tile(f"rstd{b}", [P, 1]) for b in range(2)]
        self.x_in = sem.pair("x_in")
        self.squared, self.rstd_set, self.h_set = sem("squared"), sem("rstd_set"), sem("h_set")
        self.scaled = sem("scaled")
        self.h_free = sem("h_free")
        self.gain_in, self.a_made = sem("gain_in"), sem("a_made")

    def load_rows(self, sp, io, layer, scale, shift, gain, streams=2):
        for s in range(streams):
            sp.dma_start(self.arow[s][:, :], mod_row(io["mod_d"], s, layer, scale)).then_inc(self.gain_in, 16)
            sp.dma_start(self.brow[s][:, :], mod_row(io["mod_d"], s, layer, shift)).then_inc(self.gain_in, 16)
        sp.dma_start(self.sq[:, :], gain.partition_broadcast(P)).then_inc(self.gain_in, 16)

    def make_a(self, dve, streams=2):
        dve.wait_ge(self.gain_in, 16 * (2 * streams + 1))
        for s in range(streams):
            self.nc.vector.scalar_tensor_tensor(self.arow[s][:, :], self.arow[s][:, :], 1.0, self.sq[:, :],
                                                ALU.add, ALU.mult).then_inc(self.a_made, 1)
        dve.wait_ge(self.a_made, streams)

    def load(self, sp, a, src):
        sp.wait_ge(self.scaled, a.t + 1)
        settle(sp, self.g)
        sp.dma_start(self.x[a.b][:, :], rows(src, a.t)).then_inc(self.x_in[a.b], 16)

    def square(self, act, a):
        act.wait_ge(self.x_in[a.b], 16 * (a.i + 1))
        act.wait_ge(self.squared, a.t + 1)
        self.nc.scalar.activation(self.sq[:, :], self.x[a.b][:, :], ACT.Square,
                                  accum_out=self.ssq[a.b][:, :]).then_inc(self.squared, 1)

    def root(self, pool, a):
        b = a.b
        pool.wait_ge(self.squared, a.t + 2)
        settle(pool, self.g)
        self.nc.gpsimd.tensor_scalar(self.ms[b][:, :], self.ssq[b][:, :], 1.0 / D, EPS,
                                     ALU.mult, ALU.add).then_inc(self.rstd_set, 1)
        pool.wait_ge(self.rstd_set, 2 * a.t + 1)
        self.nc.gpsimd.tensor_tensor(self.rstd[b][:, :], self.ms[b][:, :], self.g.mhalf[:, 0:1],
                                     ALU.pow).then_inc(self.rstd_set, 1)

    def scale(self, dve, a):
        b, s = a.b, a.stream()
        dve.wait_ge(self.x_in[b], 16 * (a.i + 1))
        dve.wait_ge(self.rstd_set, 2 * a.t + 2)
        dve.wait_ge(self.h_free, a.t + 1)
        self.nc.vector.scalar_tensor_tensor(self.h[b][:, :], self.x[b][:, :], self.rstd[b][:, 0:1],
                                            self.arow[s][:, :], ALU.mult, ALU.mult).then_inc(self.scaled, 1)
        dve.wait_ge(self.scaled, a.t + 3)
        self.nc.vector.tensor_tensor(self.h[b][:, :], self.h[b][:, :], self.brow[s][:, :],
                                     ALU.add).then_inc(self.h_set, 1)


def transpose_tile(nc, g, bank, src, blocks=range(KD)):
    for n, k in enumerate(blocks):
        last = nc.tensor.transpose(g.psum[:, bank + n // 4, (n % 4) * P:(n % 4 + 1) * P],
                                   src[:, k * P:(k + 1) * P], g.ident[:, :])
    return last


def conv_inputs(nc, io, g, conv):
    with ExitStack() as st:
        tile = tiles_of(nc, st, "ci")
        sem = Signals(nc, "ci")
        norm = Norm(nc, g, tile, sem)
        hT = [tile(f"hT{b}", [P, D]) for b in range(2)]
        sig = tile("sig", [P, HALF])
        u = tile("u", [P, HALF])
        hT_set, hT_out = sem("hT_set"), sem.pair("hT_out")
        proj = sem("proj")
        sig_set, uT_set, pads = sem("sig_set"), sem("uT_set"), sem("pads")
        u_set = sem("u_set")
        u_turned = sem("u_turned")
        wv = g.ring[:, :].rearrange("p (c k n) -> p c k n", c=EVC, k=KD)

        with nc.Block() as block:
            @block.sync
            def _(sp):
                norm.load_rows(sp, io, 0, SC1, SH1, io["norm1_g"][0])
                for b in range(2):
                    sp.sem_inc(hT_out[b], 16)
                    norm.load(sp, At(0, b), io["tok"])

                def step(a):
                    if a.plus(2).exists(NT):
                        norm.load(sp, a.plus(2), io["tok"])
                    if a.b == 0:
                        sp.dma_start(g.ring[:, bass.ds((a.i + C_Q) * (2 * PW), 2 * PW)],
                                     rows(io["ev_w_in"], a.i + C_Q)).then_inc(g.ev_ret_in, 16)
                    sp.wait_ge(hT_set, a.t + 1)
                    settle(sp, g)
                    sp.dma_start(rows(io["hT_d"], a.t), hT[a.b][:, :]).then_inc(hT_out[a.b], 16)
                run(sp, step, NT // 2, 0, NT // 2 - 1)
                for b in range(2):
                    sp.wait_ge(hT_out[b], 16 * (NT // 2 + 1))

            @block.scalar
            def _(act):
                act.sem_inc(norm.squared, 1)
                act.wait_ge(norm.a_made, 2)

                def copy_h(a):
                    act.wait_ge(norm.h_free, a.t + 3)
                    act.wait_ge(hT_out[a.b], 16 * (a.i + 1))
                    act.wait_ge(proj, a.t + 1)
                    nc.scalar.copy(hT[a.b][:, :], g.psum[:, 0:2, :].rearrange("p a n -> p (a n)")).then_inc(hT_set, 1)

                def copy_u(a):
                    act.wait_ge(u_turned, a.t + 2)
                    c0 = UC0 + P * (a.t - XT) if a.stream() else UX0 + P * a.t
                    nc.scalar.copy(conv.u[:, :, bass.ds(c0, P)],
                                   g.psum[:, 6 + a.b, :].rearrange("p (j n) -> p j n", j=4)).then_inc(uT_set, 1)

                def step(a):
                    if a.plus(2).exists(NT):
                        norm.square(act, a.plus(2))
                    if a.plus(1).exists(NT):
                        copy_h(a.plus(1))
                    act.wait_ge(proj, a.t + 3)
                    act.wait_ge(u_set, a.t + 1)
                    nc.scalar.activation(sig[:, :], g.psum[:, 4 + a.b, :], ACT.Sigmoid).then_inc(sig_set, 1)
                    if a.plus(-1).exists(NT):
                        copy_u(a.plus(-1))
                norm.square(act, At(0, 0))
                norm.square(act, At(0, 1))
                copy_h(At(0, 0))
                run(act, step, NT // 2, 1, XT // 2)
                copy_u(At(NT // 2 - 1, 1))

            @block.gpsimd
            def _(pool):
                for j in range(4):
                    for lo, hi in ((0, UX0), (UX0 + SEQ, UC0), (UC0 + CTX, UW)):
                        nc.gpsimd.memset(conv.u[:, j, lo:hi], 0.0).then_inc(pads, 1)
                run(pool, lambda a: norm.root(pool, a), NT // 2, 0, NT // 2)
                pool.wait_ge(pads, 12)

            @block.vector
            def _(dve):
                dve.sem_inc(norm.scaled, 2)
                dve.sem_inc(u_set, 1)
                norm.make_a(dve)
                norm.scale(dve, At(0, 0))
                norm.scale(dve, At(0, 1))

                def step(a):
                    if a.plus(2).exists(NT):
                        norm.scale(dve, a.plus(2))
                    dve.wait_ge(sig_set, a.t + 1)
                    dve.wait_ge(u_turned, a.t + 1)
                    nc.vector.tensor_tensor(u[:, :], g.psum[:, 2 + a.b, :], sig[:, :], ALU.mult).then_inc(u_set, 1)
                run(dve, step, NT // 2, 0, XT // 2 - 1)

            @block.tensor
            def _(pe):
                pe.sem_inc(norm.h_free, 2)
                pe.sem_inc(proj, 2)
                pe.sem_inc(u_turned, 1)
                pe.wait_ge(g.ident_in, 16)

                def turn_h(a):
                    pe.wait_ge(norm.h_set, a.t + 1)
                    if not (isinstance(a.i, int) and a.t == 0):
                        pe.wait_ge(hT_set, a.t)
                    transpose_tile(nc, g, 0, norm.h[a.b]).then_inc(norm.h_free, 1)

                def products(a):
                    pe.wait_ge(hT_set, a.t + 1)
                    for c, bank in ((C_BV, 2 + a.b), (C_BG, 4 + a.b)):
                        for k in range(KD):
                            last = nc.tensor.matmul(g.psum[:, bank, :], hT[a.b][:, k * P:(k + 1) * P],
                                                    wv[:, c, k, :], start=(k == 0), stop=(k == KD - 1))
                    last.then_inc(proj, 1)

                def turn_u(a):
                    pe.wait_ge(u_set, a.t + 2)
                    if not (isinstance(a.i, int) and a.t < 2):
                        pe.wait_ge(uT_set, a.t - 1)
                    transpose_tile(nc, g, 6 + a.b, u, range(4)).then_inc(u_turned, 1)

                def step(a):
                    if a.plus(1).exists(NT):
                        turn_h(a.plus(1))
                    products(a)
                    if a.plus(-1).exists(NT):
                        turn_u(a.plus(-1))
                turn_h(At(0, 0))
                pe.wait_ge(g.ev_conv_in, 32)
                run(pe, step, NT // 2, 2, NT // 2 - 1)
                turn_u(At(NT // 2 - 1, 1))
        sem.release()


def heads_view(x, n=HEADS):
    return x.rearrange("p (h d) -> p h d", h=n)


def per_head(col, width, n=HEADS):
    return col.unsqueeze(2).to_broadcast([P, n, width])


def rope_steps(nc, pool, signal, base, out, src, cs, tmp, parts, seg):
    w = 4 * seg
    c = cs[:, 0:w].unsqueeze(1).to_broadcast([P, parts, w])
    sn = cs[:, w:2 * w].rearrange("p (a s m) -> p a s m", a=2, s=2)
    sv = src.rearrange("p h (a s m) -> p h a s m", a=2, s=2)
    tv = tmp.rearrange("p h (a s m) -> p h a s m", a=2, s=2)
    pool.wait_ge(signal, base + 1)
    nc.gpsimd.tensor_tensor(out, src, c, ALU.mult).then_inc(signal, 1)
    for half in range(2):
        nc.gpsimd.tensor_tensor(tv[:, :, :, half, :], sv[:, :, :, 1 - half, :],
                                sn[:, :, half, :].unsqueeze(1).to_broadcast([P, parts, 2, seg]),
                                ALU.mult).then_inc(signal, 1)
    pool.wait_ge(signal, base + 4)
    nc.gpsimd.tensor_tensor(out, out, tmp, ALU.add).then_inc(signal, 1)


def projections(nc, io, g, conv):
    with ExitStack() as st:
        tile = tiles_of(nc, st, "pr")
        sem = Signals(nc, "pr")
        hT = [tile(f"hT{b}", [P, D]) for b in range(2)]
        cs = [tile(f"cs{b}", [P, 2 * HD]) for b in range(2)]
        rec = [tile(f"rec{b}", [P, RECW]) for b in range(2)]
        qraw, kraw, qrope, tmp = (tile(n, [P, HALF]) for n in ("qraw", "kraw", "qrope", "tmp"))
        gain = tile("gain", [P, HALF])
        taps = tile("taps", [P, 4 * TAPS])
        tapb = tile("tapb", [P, 4])
        small_in, gain_in = sem("small_in"), sem("gain_in")
        hT_in, cs_in, rec_out = sem.pair("hT_in"), sem.pair("cs_in"), sem.pair("rec_out")
        hT_used = sem("hT_used")
        proj = sem("proj")
        evac = sem("evac")
        rope = sem("rope")
        gated, turned = sem("gated"), sem("turned")
        turn_out = sem("turn_out")
        conv_x, conv_c = sem("conv_x"), sem("conv_c")
        wv = g.ring[:, :].rearrange("p (c k n) -> p c k n", c=EVC, k=KD)
        order = (C_Q, C_K, C_V, C_GF, C_GB)
        nch = len(order)

        def part(b, r):
            return rec[b][:, r * HALF:(r + 1) * HALF]

        with nc.Block() as block:
            @block.sync
            def _(sp):
                sp.dma_start(taps[:, :], io["conv_w"]).then_inc(small_in, 16)
                sp.dma_start(tapb[:, :], io["conv_b"]).then_inc(small_in, 16)
                sp.dma_start(gain[:, :], io["ret_gn_g"].partition_broadcast(P)).then_inc(gain_in, 16)
                for b in range(2):
                    sp.sem_inc(rec_out[b], 16)

                def load(a):
                    sp.wait_ge(hT_used, a.t + 1)
                    settle(sp, g)
                    sp.dma_start(hT[a.b][:, :], rows(io["hT_d"], a.t)).then_inc(hT_in[a.b], 16)
                    if not (isinstance(a.i, int) and a.i == 0):
                        sp.wait_ge(rope, 8 * (a.t - 1) + 1)
                    settle(sp, g)
                    sp.dma_start(cs[a.b][:, :], rows(io["rope_ret"], a.t)).then_inc(cs_in[a.b], 16)

                def step(a):
                    if a.plus(2).exists(NT):
                        load(a.plus(2))
                    sp.wait_ge(evac, nch * a.t + 2 * nch)
                    sp.wait_ge(rope, 8 * a.t + 9)
                    sp.wait_ge(gated, 2 * a.t + 2)
                    settle(sp, g)
                    sp.wait_ge(turn_out, 2 * a.t + 4)
                    settle(sp, g)
                    sp.dma_start(rows(io["rec_d"], a.t + CT), rec[a.b][:, :]).then_inc(rec_out[a.b], 16)
                    if a.stream():
                        sp.dma_start(rows(io["rec_d"], a.t - XT), rec[a.b][:, :]).then_inc(rec_out[a.b], 16)
                load(At(0, 0))
                load(At(0, 1))
                run(sp, step, NT // 2, 0, XT // 2)
                for b in range(2):
                    sp.wait_ge(rec_out[b], 16 * (NT // 2 + 2))

            @block.tensor
            def _(pe):
                pe.sem_inc(hT_used, 2)
                pe.wait_ge(g.ev_ret_in, 16 * nch)

                def step(a):
                    pe.wait_ge(hT_in[a.b], 16 * (a.i + 1))
                    for n, c in enumerate(order):
                        pe.wait_ge(evac, nch * a.t + n + 1)
                        for k in range(KD):
                            last = nc.tensor.matmul(g.psum[:, n, :], hT[a.b][:, k * P:(k + 1) * P], wv[:, c, k, :],
                                                    start=(k == 0), stop=(k == KD - 1))
                        last.then_inc(proj, 1)
                    pe.wait_ge(rope, 8 * a.t + 5)
                    pe.wait_ge(turn_out, 2 * a.t + 1)
                    transpose_tile(nc, g, 5, qrope, range(4)).then_inc(turned, 1)
                    pe.wait_ge(rope, 8 * a.t + 9)
                    pe.wait_ge(turn_out, 2 * a.t + 2)
                    transpose_tile(nc, g, 6, part(a.b, R_K), range(4)).then_inc(turned, 1)
                    pe.wait_ge(proj, nch * (a.t + 1))
                    pe.sem_inc(hT_used, 1)
                run(pe, step, NT // 2, 0, NT // 2)

            @block.scalar
            def _(act):
                act.sem_inc(evac, nch)
                act.sem_inc(turn_out, 2)

                def step(a):
                    b = a.b
                    act.wait_ge(proj, nch * a.t + 1)
                    act.wait_ge(rope, 8 * a.t + 1)
                    nc.scalar.copy(qraw[:, :], g.psum[:, 0, :]).then_inc(evac, 1)
                    act.wait_ge(proj, nch * a.t + 2)
                    nc.scalar.activation(kraw[:, :], g.psum[:, 1, :], ACT.Copy, scale=HD ** -0.5).then_inc(evac, 1)
                    act.wait_ge(rec_out[b], 16 * (a.i + 1))
                    act.wait_ge(proj, nch * a.t + 3)
                    nc.scalar.copy(part(b, R_V), g.psum[:, 2, :]).then_inc(evac, 1)
                    for n, r in ((3, R_GF), (4, R_GB)):
                        act.wait_ge(proj, nch * a.t + n + 1)
                        nc.scalar.activation(part(b, r), g.psum[:, n, :], ACT.Silu).then_inc(evac, 1)
                    for n, r in ((0, R_QT), (1, R_KT)):
                        act.wait_ge(turned, 2 * a.t + n + 1)
                        nc.scalar.copy(part(b, r), g.psum[:, 5 + n, :]).then_inc(turn_out, 1)
                run(act, step, NT // 2, 0, NT // 2)

            @block.gpsimd
            def _(pool):
                pool.sem_inc(rope, 1)
                pool.wait_ge(gain_in, 16)

                def step(a):
                    b = a.b
                    pool.wait_ge(evac, nch * a.t + nch + 1)
                    pool.wait_ge(cs_in[b], 16 * (a.i + 1))
                    if not (isinstance(a.i, int) and a.t == 0):
                        pool.wait_ge(turned, 2 * a.t - 1)
                    rope_steps(nc, pool, rope, 8 * a.t, heads_view(qrope[:, :]), heads_view(qraw[:, :]), cs[b],
                               heads_view(tmp[:, :]), HEADS, HD // 4)
                    pool.wait_ge(evac, nch * a.t + nch + 2)
                    pool.wait_ge(rec_out[b], 16 * (a.i + 1))
                    rope_steps(nc, pool, rope, 8 * a.t + 4, heads_view(part(b, R_K)), heads_view(kraw[:, :]), cs[b],
                               heads_view(tmp[:, :]), HEADS, HD // 4)
                    for n, r in ((3, R_GF), (4, R_GB)):
                        pool.wait_ge(evac, nch * a.t + nch + n + 1)
                        nc.gpsimd.tensor_tensor(part(b, r), part(b, r), gain[:, :], ALU.mult).then_inc(gated, 1)
                run(pool, step, NT // 2, 1, NT // 2)

            @block.vector
            def _(dve):
                dve.wait_ge(small_in, 32)
                uf = conv.u[:, :, :].rearrange("p j n -> p (j n)")
                yf = conv.y[:, :, :].rearrange("p j n -> p (j n)")
                with dve.Fori(0, 4) as j:
                    for tap in range(TAPS):
                        w = taps[:, bass.ds(j * TAPS + tap, 1)]
                        for done, u0, y0, n in ((conv_x, 0, 0, SEQ), (conv_c, UC0 - PADT, SEQ, CTX)):
                            ys = yf[:, bass.ds(j * TOK + y0, n)]
                            us = uf[:, bass.ds(j * UW + u0 + tap, n)]
                            if tap == 0:
                                nc.vector.tensor_scalar(ys, us, w, tapb[:, bass.ds(j, 1)],
                                                        ALU.mult, ALU.add).then_inc(done, 1)
                            else:
                                dve.wait_ge(done, j * TAPS + tap)
                                nc.vector.scalar_tensor_tensor(ys, us, w, ys, ALU.mult, ALU.add).then_inc(done, 1)
                dve.wait_ge(conv_x, 4 * TAPS)
                dve.wait_ge(conv_c, 4 * TAPS)
        sem.release()


def retention(nc, io, g, conv):
    with ExitStack() as st:
        tile = tiles_of(nc, st, "re")
        sem = Signals(nc, "re")
        dirs = range(2)
        carve = Carve(g.ring, WOUT)
        rec = [[carve(5 * HALF) for b in range(2)] for d in dirs]
        table = tile("table", [P, 6 * P + 2])
        lg, lga, decay = (tile(n, [P, 2 * HEADS]) for n in ("lg", "lga", "decay"))
        intra = [carve(HALF) for d in dirs]
        xi = [carve(HALF) for d in dirs]
        zeta = tile("zeta", [P, 2 * HEADS])
        state = [carve(HALF) for d in dirs]
        sm = [carve(HALF) for d in dirs]
        qx = [carve(HALF) for d in dirs]
        kz = [carve(HALF) for d in dirs]
        xh = [carve(HALF) for d in dirs]
        ret = [[tile(f"ret{d}{b}", [P, HALF]) for b in range(2)] for d in dirs]
        stats = [tile(f"stats{d}", [P, HEADS, 6]) for d in dirs]
        mv = [tile(f"mv{d}", [P, HEADS, 2]) for d in dirs]
        ve = [tile(f"ve{d}", [P, HEADS]) for d in dirs]
        rs = [tile(f"rs{d}", [P, HEADS]) for d in dirs]
        nm = [tile(f"nm{d}", [P, HEADS]) for d in dirs]
        ln = tile("ln", [P, 8])
        ys, yn = tile("ys", [P, HALF]), tile("yn", [P, HALF])
        mixc = [tile(f"mixc{b}", [P, HALF]) for b in range(2)]
        cst, cmv, cve, crs, cnm = (tile(n, [P, w]) for n, w in (("cst", 6), ("cmv", 2), ("cve", 1), ("crs", 1), ("cnm", 1)))

        table_in, lg_in, ln_in, setup = sem("table_in"), sem("lg_in"), sem("ln_in"), sem("setup")
        tables_made = sem("tables_made")
        rec_in = [sem.pair(f"rec_in{d}") for d in dirs]
        ret_out = [sem.pair(f"ret_out{d}") for d in dirs]
        scored = [sem(f"scored{d}") for d in dirs]
        masked = [sem(f"masked{d}") for d in dirs]
        qx_set = [sem(f"qx_set{d}") for d in dirs]
        kz_set = [sem(f"kz_set{d}") for d in dirs]
        kv_sum = [sem(f"kv_sum{d}") for d in dirs]
        out_sum = [sem(f"out_sum{d}") for d in dirs]
        state_set = [sem(f"state_set{d}") for d in dirs]
        stat = [sem(f"stat{d}") for d in dirs]
        root = [sem(f"root{d}") for d in dirs]
        shift = [sem(f"shift{d}") for d in dirs]
        normed = [sem(f"normed{d}") for d in dirs]
        gated = [sem(f"gated{d}") for d in dirs]
        c_cut, c_turned, c_stat, c_root, c_shift, c_normed, c_back, c_done = (
            sem("c_" + n) for n in ("cut", "turned", "stat", "root", "shift", "normed", "back", "done"))
        mixc_out = sem.pair("mixc_out")

        with nc.Block() as block:
            @block.sync
            def _(sp):
                sp.dma_start(table[:, :], io["ret_table"]).then_inc(table_in, 16)
                sp.dma_start(lg[:, :], io["ret_logit"].partition_broadcast(P)).then_inc(lg_in, 16)
                sp.dma_start(ln[:, :], io["conv_ln"]).then_inc(ln_in, 16)
                sp.dma_start(g.ring[:, 0:WOUT], io["ev_w_out"]).then_inc(g.wout_in, 16)
                sp.dma_start(g.router[:, :], io["router_w"][0]).then_inc(g.wout_in, 16)

                def load(a):
                    for d in dirs:
                        r = a.t if d == 0 else NT + 1 - a.t
                        sp.wait_ge(gated[d], a.t + 1)
                        settle(sp, g)
                        src = rows(io["rec_d"], r)
                        sp.dma_start(rec[d][a.b][:, 0:4 * HALF], src[:, 0:4 * HALF]).then_inc(rec_in[d][a.b], 16)
                        gcol = (R_GF + d) * HALF
                        sp.dma_start(rec[d][a.b][:, 4 * HALF:], src[:, gcol:gcol + HALF]).then_inc(rec_in[d][a.b], 16)
                for d in dirs:
                    sp.sem_inc(ret_out[d][0], 16)
                    sp.sem_inc(ret_out[d][1], 16)
                sp.sem_inc(mixc_out[0], 16)
                sp.sem_inc(mixc_out[1], 16)

                def step(a):
                    if a.plus(2).exists(NT):
                        load(a.plus(2))
                    sp.wait_ge(c_done, a.t + 1)
                    settle(sp, g)
                    sp.dma_start(rows(io["mix_d"], a.t)[:, HALF:D], mixc[a.b][:, :]).then_inc(mixc_out[a.b], 16)
                    for d in dirs:
                        r = a.t if d == 0 else NT + 1 - a.t
                        sp.wait_ge(gated[d], a.t + 3)
                        settle(sp, g)
                        sp.dma_start(rows(io["ret_d"][d], r), ret[d][a.b][:, :]).then_inc(ret_out[d][a.b], 16)
                load(At(0, 0))
                load(At(0, 1))
                run(sp, step, NT // 2, 0, NT // 2 - 1)
                for b in range(2):
                    sp.wait_ge(mixc_out[b], 16 * (NT // 2 + 1))
                    for d in dirs:
                        sp.wait_ge(ret_out[d][b], 16 * (NT // 2 + 1))

            @block.tensor
            def _(pe):
                for d in dirs:
                    pe.sem_inc(kv_sum[d], 1)
                    pe.sem_inc(out_sum[d], 1)

                def hs(x, h, at=0):
                    return x[:, at + h * HD:at + (h + 1) * HD]

                def step(a):
                    for d in dirs:
                        r = rec[d][a.b]
                        pe.wait_ge(rec_in[d][a.b], 32 * (a.i + 1))
                        pe.wait_ge(masked[d], a.t + 1)
                        for h in range(HEADS):
                            last = nc.tensor.matmul(g.psum[:, d, h * P:(h + 1) * P], hs(r, h, R_KT * HALF),
                                                    hs(r, h, R_QT * HALF), start=True, stop=True)
                        last.then_inc(scored[d], 1)
                    pe.wait_ge(c_cut, a.t + 1)
                    if not (isinstance(a.i, int) and a.t == 0):
                        pe.wait_ge(c_normed, a.t)
                    transpose_tile(nc, g, 6, ys, range(4)).then_inc(c_turned, 1)
                    for d in dirs:
                        pe.wait_ge(kz_set[d], a.t + 1)
                        pe.wait_ge(state_set[d], a.t + 1)
                        for h in range(HEADS):
                            last = nc.tensor.matmul(g.psum[:, 2 + d, h * P:(h + 1) * P], hs(kz[d], h),
                                                    hs(rec[d][a.b], h, R_V * HALF), start=True, stop=True)
                        last.then_inc(kv_sum[d], 1)
                    for d in dirs:
                        pe.wait_ge(masked[d], a.t + 2)
                        pe.wait_ge(qx_set[d], a.t + 1)
                        pe.wait_ge(normed[d], a.t + 1)
                        for h in range(HEADS):
                            o = g.psum[:, 4 + d, h * P:(h + 1) * P]
                            nc.tensor.matmul(o, hs(sm[d], h), hs(rec[d][a.b], h, R_V * HALF), start=True, stop=False)
                            last = nc.tensor.matmul(o, hs(qx[d], h), hs(state[d], h), start=False, stop=True)
                        last.then_inc(out_sum[d], 1)
                    pe.wait_ge(c_normed, a.t + 1)
                    if not (isinstance(a.i, int) and a.t == 0):
                        pe.wait_ge(c_done, a.t)
                    transpose_tile(nc, g, 7, yn, range(4)).then_inc(c_back, 1)
                run(pe, step, NT // 2, 1, NT // 2)

            @block.vector
            def _(dve):
                dve.wait_ge(lg_in, 16)
                nc.vector.tensor_scalar(lga[:, :], lg[:, :], -1.0, None, ALU.mult).then_inc(setup, 1)
                dve.wait_ge(setup, 1)
                nc.vector.tensor_tensor(lga[:, :], lga[:, :], lg[:, :], ALU.min).then_inc(setup, 1)
                dve.wait_ge(setup, 3)
                nc.vector.tensor_scalar(lga[:, :], lga[:, :], 1.0, None, ALU.add).then_inc(setup, 1)
                dve.wait_ge(setup, 5)
                nc.vector.tensor_scalar(lg[:, :], lg[:, :], 0.0, None, ALU.min).then_inc(setup, 1)
                dve.wait_ge(setup, 6)
                nc.vector.tensor_tensor(lg[:, :], lg[:, :], lga[:, :], ALU.subtract).then_inc(setup, 1)
                for d in dirs:
                    nc.vector.memset(state[d][:, :], 0.0).then_inc(state_set[d], 1)
                dve.wait_ge(tables_made, 1)
                for d in dirs:
                    m = table[:, (1 + 2 * d) * P:(2 + 2 * d) * P].unsqueeze(1).to_broadcast([P, HEADS, P])
                    nc.vector.tensor_tensor(heads_view(intra[d][:, :]), heads_view(intra[d][:, :]), m,
                                            ALU.mult).then_inc(tables_made, 1)
                dve.wait_ge(tables_made, 3)
                for d in dirs:
                    dve.sem_inc(masked[d], 1)

                def step(a):
                    for d in dirs:
                        dve.wait_ge(scored[d], a.t + 1)
                        dve.wait_ge(out_sum[d], a.t + 1)
                        nc.vector.tensor_tensor(sm[d][:, :], g.psum[:, d, :], intra[d][:, :],
                                                ALU.mult).then_inc(masked[d], 1)
                        nc.vector.tensor_tensor(qx[d][:, :], rec[d][a.b][:, R_QT * HALF:(R_QT + 1) * HALF], xi[d][:, :],
                                                ALU.mult).then_inc(qx_set[d], 1)
                    dve.wait_ge(c_turned, a.t + 1)
                    nc.vector.bn_stats(cst[:, :], g.psum[:, 6, :]).then_inc(c_stat, 1)
                    dve.wait_ge(c_stat, 2 * a.t + 1)
                    if not (isinstance(a.i, int) and a.t == 0):
                        dve.wait_ge(c_shift, a.t)
                    settle(dve, g)
                    nc.vector.bn_aggr(cmv[:, :], cst[:, :]).then_inc(c_stat, 1)
                    dve.wait_ge(c_root, 2 * a.t + 2)
                    nc.vector.scalar_tensor_tensor(cnm[:, :], cmv[:, 0:1], -1.0, crs[:, :],
                                                   ALU.mult, ALU.mult).then_inc(c_shift, 1)
                    for d in dirs:
                        dve.wait_ge(out_sum[d], a.t + 2)
                        for h in range(HEADS):
                            nc.vector.bn_stats(stats[d][:, h, :], g.psum[:, 4 + d, h * P:(h + 1) * P]).then_inc(
                                stat[d], 1)
                        dve.wait_ge(stat[d], 2 * HEADS * a.t + HEADS)
                        settle(dve, g)
                        for h in range(HEADS):
                            nc.vector.bn_aggr(mv[d][:, h, :], stats[d][:, h, :]).then_inc(stat[d], 1)
                    for d in dirs:
                        dve.wait_ge(kv_sum[d], a.t + 2)
                        for h in range(HEADS):
                            c = slice(h * P, (h + 1) * P)
                            last = nc.vector.scalar_tensor_tensor(state[d][:, c], state[d][:, c],
                                                                  decay[:, d * HEADS + h:d * HEADS + h + 1],
                                                                  g.psum[:, 2 + d, c], ALU.mult, ALU.add)
                        last.then_inc(state_set[d], 1)
                        dve.wait_ge(root[d], 2 * a.t + 2)
                        dve.wait_ge(normed[d], a.t + 1)
                        nc.vector.scalar_tensor_tensor(nm[d][:, :], mv[d][:, :, 0], -1.0, rs[d][:, :],
                                                       ALU.mult, ALU.mult).then_inc(shift[d], 1)
                    for d in dirs:
                        dve.wait_ge(shift[d], a.t + 1)
                    dve.wait_ge(c_shift, a.t + 1)
                    for d in dirs:
                        dve.wait_ge(state_set[d], a.t + 2)
                run(dve, step, NT // 2, 1, NT // 2)

            @block.gpsimd
            def _(pool):
                for d in dirs:
                    pool.sem_inc(gated[d], 2)
                pool.wait_ge(tables_made, 3)

                def decayed_keys(a):
                    for d in dirs:
                        r = rec[d][a.b]
                        pool.wait_ge(rec_in[d][a.b], 32 * (a.i + 1))
                        pool.wait_ge(kv_sum[d], a.t + 1)
                        nc.gpsimd.tensor_tensor(heads_view(kz[d][:, :]),
                                                heads_view(r[:, R_K * HALF:(R_K + 1) * HALF]),
                                                per_head(zeta[:, d * HEADS:(d + 1) * HEADS], HD),
                                                ALU.mult).then_inc(kz_set[d], 1)

                def step(a):
                    pool.wait_ge(c_stat, 2 * a.t + 2)
                    settle(pool, g)
                    nc.gpsimd.tensor_scalar(cve[:, :], cmv[:, 1:2], EPS, None, ALU.add).then_inc(c_root, 1)
                    pool.wait_ge(c_root, 2 * a.t + 1)
                    if not (isinstance(a.i, int) and a.t == 0):
                        pool.wait_ge(c_normed, a.t)
                    nc.gpsimd.tensor_tensor(crs[:, :], cve[:, :], g.mhalf[:, 0:1], ALU.pow).then_inc(c_root, 1)
                    for d in dirs:
                        pool.wait_ge(stat[d], 2 * HEADS * (a.t + 1))
                        settle(pool, g)
                        nc.gpsimd.tensor_scalar(ve[d][:, :], mv[d][:, :, 1], EPS, None, ALU.add).then_inc(root[d], 1)
                        pool.wait_ge(root[d], 2 * a.t + 1)
                        pool.wait_ge(normed[d], a.t + 1)
                        nc.gpsimd.tensor_tensor(rs[d][:, :], ve[d][:, :], g.mhalf[:, 0:HEADS],
                                                ALU.pow).then_inc(root[d], 1)
                    if a.plus(1).exists(NT):
                        decayed_keys(a.plus(1))
                    for d in dirs:
                        pool.wait_ge(normed[d], a.t + 2)
                        pool.wait_ge(ret_out[d][a.b], 16 * (a.i + 1))
                        nc.gpsimd.tensor_tensor(ret[d][a.b][:, :], xh[d][:, :], rec[d][a.b][:, 4 * HALF:],
                                                ALU.mult).then_inc(gated[d], 1)
                decayed_keys(At(0, 0))
                run(pool, step, NT // 2, 1, NT // 2 - 1)

            @block.scalar
            def _(act):
                act.wait_ge(setup, 2)
                nc.scalar.activation(lga[:, :], lga[:, :], ACT.Exp).then_inc(setup, 1)
                act.wait_ge(setup, 4)
                nc.scalar.activation(lga[:, :], lga[:, :], ACT.Ln).then_inc(setup, 1)
                act.wait_ge(setup, 7)
                act.wait_ge(table_in, 16)
                for d in dirs:
                    for h in range(HEADS):
                        n = d * HEADS + h
                        col = lg[:, n:n + 1]
                        c = slice(h * P, (h + 1) * P)
                        nc.scalar.activation(intra[d][:, c], table[:, 2 * d * P:(2 * d + 1) * P], ACT.Exp, scale=col)
                        nc.scalar.activation(xi[d][:, c], table[:, (4 + d) * P:(5 + d) * P], ACT.Exp, scale=col)
                        nc.scalar.activation(zeta[:, n:n + 1], table[:, 6 * P + d:6 * P + d + 1], ACT.Exp, scale=col)
                nc.scalar.activation(decay[:, :], lg[:, :], ACT.Exp, scale=float(P)).then_inc(tables_made, 1)
                act.wait_ge(ln_in, 16)
                for d in dirs:
                    act.sem_inc(normed[d], 1)

                def cut(a):
                    if not (isinstance(a.i, int) and a.t == 0):
                        act.wait_ge(c_turned, a.t)
                    nc.scalar.copy(ys[:, :].rearrange("p (j n) -> p j n", j=4),
                                   conv.y[:, :, bass.ds(P * a.t, P)]).then_inc(c_cut, 1)

                def step(a):
                    act.wait_ge(c_shift, a.t + 1)
                    if not (isinstance(a.i, int) and a.t == 0):
                        act.wait_ge(c_back, a.t)
                    nc.scalar.activation(yn[:, :], g.psum[:, 6, :], ACT.Identity, bias=cnm[:, 0:1],
                                         scale=crs[:, 0:1]).then_inc(c_normed, 1)
                    if a.plus(1).exists(NT):
                        cut(a.plus(1))
                    for d in dirs:
                        act.wait_ge(shift[d], a.t + 1)
                        act.wait_ge(gated[d], a.t + 2)
                        for h in range(HEADS):
                            c = slice(h * P, (h + 1) * P)
                            last = nc.scalar.activation(xh[d][:, c], g.psum[:, 4 + d, c], ACT.Identity,
                                                        bias=nm[d][:, h:h + 1], scale=rs[d][:, h:h + 1])
                        last.then_inc(normed[d], 1)
                    act.wait_ge(c_back, a.t + 1)
                    act.wait_ge(mixc_out[a.b], 16 * (a.i + 1))
                    for j in range(4):
                        c = slice(j * P, (j + 1) * P)
                        last = nc.scalar.activation(mixc[a.b][:, c], g.psum[:, 7, c], ACT.Silu,
                                                    bias=ln[:, 4 + j:5 + j], scale=ln[:, j:j + 1])
                    last.then_inc(c_done, 1)
                cut(At(0, 0))
                run(act, step, NT // 2, 1, NT // 2 - 1)
        sem.release()


def mixer_out(nc, io, g, layer):
    even = layer == 0
    nt = NT if even else XT
    streams = 2 if even else 1
    src = io["tok"] if even else io["x1_d"]
    res = io["x1_d"] if even else io["out"]
    with ExitStack() as st:
        tile = tiles_of(nc, st, f"mo{layer}")
        sem = Signals(nc, f"mo{layer}")
        carve = Carve(g.ring, WOUT)
        arow, brow, grow = ([carve(D) for s in range(streams)] for n in range(3))
        sq = carve(D)
        mix = [carve(D) for b in range(2)]
        x = [carve(D) for b in range(2)]
        h = [carve(D) for b in range(2)]
        y = carve(D)
        hT = carve(D)
        rf, rb = ([carve(HALF) for b in range(2)] for n in range(2))
        rsum = carve(HALF)
        w_high, w_low = tile("w_high", [P, WOUT], F32R), tile("w_low", [P, WOUT], F32R)
        mix_high, mix_low = ([tile(f"{n}{b}", [P, D], F32R) for b in range(2)] for n in ("mix_high", "mix_low"))
        ssq, ms, rstd, nmax, esum, rsm = (tile(n, [P, 1]) for n in ("ssq", "ms", "rstd", "nmax", "esum", "rsm"))
        ex, aff = tile("ex", [P, NE]), tile("aff", [P, NE])
        gain_in, a_made = sem("gain_in"), sem("a_made")
        x_in, mix_in, r_in = sem.pair("x_in"), sem.pair("mix_in"), sem.pair("r_in")
        x_out, h_out = sem.pair("x_out"), sem.pair("h_out")
        r_sum = sem("r_sum")
        r_turned = sem("r_turned")
        mix_set = sem("mix_set")
        wh_set, wl_set = sem("wh_set"), sem("wl_set")
        high_set = sem("high_set")
        split = sem("split")
        summed = sem("summed")
        y_set, x_set = sem("y_set"), sem("x_set")
        squared, root = sem("squared"), sem("root")
        scaled, h_set = sem("scaled"), sem("h_set")
        h_turned = sem("h_turned")
        hT_set, routed = sem("hT_set"), sem("routed")
        max_set, exp_set, inv_set, aff_set = sem("max_set"), sem("exp_set"), sem("inv_set"), sem("aff_set")
        aff_turned, affT_set = sem("aff_turned"), sem("affT_set")
        wh, wl = (w[:, :].rearrange("p (k n) -> p k n", k=KD) for w in (w_high, w_low))
        w_pieces = [slice(n * WOUT // 4, (n + 1) * WOUT // 4) for n in range(4)]

        def later(a, n=0):
            return not (isinstance(a.i, int) and a.t <= n)

        with nc.Block() as block:
            @block.sync
            def _(sp):
                for s in range(streams):
                    for dst, which in ((arow, SC2), (brow, SH2), (grow, G1)):
                        sp.dma_start(dst[s], mod_row(io["mod_d"], s, layer, which)).then_inc(gain_in, 16)
                sp.dma_start(sq, io["norm2_g"][layer].partition_broadcast(P)).then_inc(gain_in, 16)
                for b in range(2):
                    sp.sem_inc(x_out[b], 16)
                    sp.sem_inc(h_out[b], 16)

                def load_mix(a):
                    b = a.b
                    if even:
                        if later(a, 1):
                            sp.wait_ge(r_sum, a.t - 1)
                            settle(sp, g)
                        rt = a.t - XT if a.stream() else a.t + CT
                        sp.dma_start(rf[b], rows(io["ret_d"][0], rt)).then_inc(r_in[b], 16)
                        sp.dma_start(rb[b], rows(io["ret_d"][1], a.t + CT)).then_inc(r_in[b], 16)
                    sp.wait_ge(split, a.t + 1)
                    settle(sp, g)
                    if even:
                        sp.dma_start(mix[b][:, HALF:D], rows(io["mix_d"], a.t)[:, HALF:D]).then_inc(mix_in[b], 16)
                    else:
                        sp.dma_start(mix[b], rows(io["mix_d"], a.t)).then_inc(mix_in[b], 16)

                def load_x(a):
                    sp.wait_ge(x_out[a.b], 16 * (a.i + 1))
                    settle(sp, g)
                    if later(a, 1):
                        sp.wait_ge(scaled, a.t - 1)
                    settle(sp, g)
                    sp.dma_start(x[a.b], rows(src, a.t)).then_inc(x_in[a.b], 16)

                def step(a):
                    if a.plus(2).exists(nt):
                        load_mix(a.plus(2))
                    sp.wait_ge(x_set, a.t + 1)
                    settle(sp, g)
                    sp.dma_start(rows(res, a.t), x[a.b]).then_inc(x_out[a.b], 16)
                    sp.wait_ge(h_set, a.t + 1)
                    settle(sp, g)
                    sp.dma_start(rows(io["h_d"], a.t), h[a.b]).then_inc(h_out[a.b], 16)
                    if a.plus(2).exists(nt):
                        load_x(a.plus(2))
                for b in range(2):
                    load_mix(At(0, b))
                for b in range(2):
                    load_x(At(0, b))
                run(sp, step, nt // 2, 0, XT // 2 - 1)
                for b in range(2):
                    sp.wait_ge(x_out[b], 16 * (nt // 2 + 1))
                    sp.wait_ge(h_out[b], 16 * (nt // 2 + 1))

            @block.tensor
            def _(pe):
                pe.sem_inc(r_turned, 1)
                pe.sem_inc(summed, 2)
                pe.sem_inc(h_turned, 2)
                pe.wait_ge(g.wout_in, g.wout_count[layer])
                pe.wait_ge(wl_set, 4)

                def turn_r(a):
                    pe.wait_ge(r_sum, a.t + 1)
                    if later(a):
                        pe.wait_ge(mix_set, a.t)
                    transpose_tile(nc, g, 0, rsum, range(4)).then_inc(r_turned, 1)

                def step(a):
                    for c in range(2):
                        if c == 1 and even and a.plus(1).exists(nt):
                            turn_r(a.plus(1))
                        if a.exists(nt):
                            if c == 0:
                                pe.wait_ge(split, a.t + 3)
                                if later(a, 1):
                                    pe.wait_ge(y_set, a.t - 1)
                            products = ((mix_high, wh), (mix_high, wl), (mix_low, wh))
                            for k in range(KD):
                                for n, (x_part, w_part) in enumerate(products):
                                    last = nc.tensor.matmul(g.psum[:, 1 + 2 * a.b + c, :],
                                                            x_part[a.b][:, k * P:(k + 1) * P],
                                                            w_part[:, k, c * BANK:(c + 1) * BANK],
                                                            start=(k == 0 and n == 0), stop=(k == KD - 1 and n == 2))
                            if c == 1:
                                last.then_inc(summed, 1)
                        p = a.plus(-1)
                        if c == 0 and p.exists(nt):
                            pe.wait_ge(h_set, p.t + 1)
                            if later(p):
                                pe.wait_ge(hT_set, p.t)
                            transpose_tile(nc, g, 5, h[p.b]).then_inc(h_turned, 1)
                        p = a.plus(-2)
                        if c == 0 and p.exists(nt):
                            pe.wait_ge(aff_set, p.t + 1)
                            nc.tensor.transpose(g.psum[0:NE, 7, P:2 * P], aff[:, :], g.ident[:, :]).then_inc(
                                aff_turned, 1)
                    p = a.plus(-1)
                    if p.exists(nt):
                        pe.wait_ge(hT_set, p.t + 1)
                        if later(p):
                            pe.wait_ge(affT_set, p.t)
                        for k in range(KD):
                            last = nc.tensor.matmul(g.psum[:, 7, 0:NE], hT[:, k * P:(k + 1) * P],
                                                    g.router[:, k * NE:(k + 1) * NE], start=(k == 0), stop=(k == KD - 1))
                        last.then_inc(routed, 1)
                if even:
                    turn_r(At(0, 0))
                run(pe, step, nt // 2 + 1, 2, XT // 2 - 1)

            @block.vector
            def _(dve):
                dve.sem_inc(split, 2)
                for n, c in enumerate(w_pieces):
                    dve.wait_ge(wh_set, n + 1)
                    nc.vector.tensor_tensor(w_low[:, c], g.ring[:, c], w_high[:, c].bitcast(F32),
                                            ALU.subtract).then_inc(wl_set, 1)

                def low(a):
                    dve.wait_ge(high_set, a.t + 1)
                    nc.vector.tensor_tensor(mix_low[a.b][:, :], mix[a.b], mix_high[a.b][:, :].bitcast(F32),
                                            ALU.subtract).then_inc(split, 1)
                low(At(0, 0))
                dve.wait_ge(gain_in, 16 * (3 * streams + 1))
                for s in range(streams):
                    nc.vector.scalar_tensor_tensor(arow[s], arow[s], 1.0, sq, ALU.add, ALU.mult).then_inc(a_made, 1)
                dve.wait_ge(a_made, streams)

                def step(a):
                    b, s = a.b, a.stream()
                    if a.plus(1).exists(nt):
                        low(a.plus(1))
                    if a.exists(nt):
                        dve.wait_ge(summed, a.t + 3)
                        if later(a):
                            dve.wait_ge(x_set, a.t)
                        banks = g.psum[:, 1 + 2 * b:3 + 2 * b, :].rearrange("p a n -> p (a n)")
                        nc.vector.tensor_tensor(y, banks, grow[s], ALU.mult).then_inc(y_set, 1)
                        dve.wait_ge(y_set, a.t + 1)
                        dve.wait_ge(x_in[b], 16 * (a.i + 1))
                        nc.vector.tensor_tensor(x[b], x[b], y, ALU.add).then_inc(x_set, 1)
                    p = a.plus(-1)
                    if p.exists(nt):
                        dve.wait_ge(routed, p.t + 1)
                        nc.vector.tensor_reduce(nmax[:, :], g.psum[:, 7, 0:NE], AX.X, ALU.max,
                                                negate=True).then_inc(max_set, 1)
                    if a.exists(nt):
                        dve.wait_ge(root, 2 * a.t + 2)
                        dve.wait_ge(h_turned, a.t + 1)
                        dve.wait_ge(h_out[b], 16 * (a.i + 1))
                        nc.vector.scalar_tensor_tensor(h[b], x[b], rstd[:, 0:1], arow[s], ALU.mult,
                                                       ALU.mult).then_inc(scaled, 1)
                        dve.wait_ge(scaled, a.t + 1)
                        nc.vector.tensor_tensor(h[b], h[b], brow[s], ALU.add).then_inc(h_set, 1)
                    if p.exists(nt):
                        dve.wait_ge(exp_set, p.t + 1)
                        nc.vector.reciprocal(rsm[:, :], esum[:, :]).then_inc(inv_set, 1)
                        dve.wait_ge(inv_set, p.t + 1)
                        if later(p):
                            dve.wait_ge(aff_turned, p.t)
                        nc.vector.tensor_scalar(aff[:, :], ex[:, :], rsm[:, 0:1], None, ALU.mult).then_inc(aff_set, 1)
                run(dve, step, nt // 2 + 1, 1, nt // 2 - 1)

            @block.gpsimd
            def _(pool):
                def add(a):
                    pool.wait_ge(r_in[a.b], 32 * (a.i + 1))
                    pool.wait_ge(r_turned, a.t + 1)
                    nc.gpsimd.tensor_tensor(rsum, rf[a.b], rb[a.b], ALU.add).then_inc(r_sum, 1)

                def step(a):
                    if even and a.plus(1).exists(nt):
                        add(a.plus(1))
                    pool.wait_ge(squared, a.t + 1)
                    settle(pool, g)
                    nc.gpsimd.tensor_scalar(ms[:, :], ssq[:, :], 1.0 / D, EPS, ALU.mult, ALU.add).then_inc(root, 1)
                    pool.wait_ge(root, 2 * a.t + 1)
                    if later(a):
                        pool.wait_ge(scaled, a.t)
                    nc.gpsimd.tensor_tensor(rstd[:, :], ms[:, :], g.mhalf[:, 0:1], ALU.pow).then_inc(root, 1)
                if even:
                    add(At(0, 0))
                run(pool, step, nt // 2, 1, nt // 2 - 1)

            @block.scalar
            def _(act):
                act.wait_ge(g.wout_in, g.wout_count[layer])
                for n, c in enumerate(w_pieces):
                    nc.scalar.copy(w_high[:, c], g.ring[:, c]).then_inc(wh_set, 1)

                def copy_r(a):
                    act.wait_ge(r_turned, a.t + 2)
                    act.wait_ge(split, a.t + 1)
                    nc.scalar.copy(mix[a.b][:, 0:HALF], g.psum[:, 0, :]).then_inc(mix_set, 1)

                def high(a):
                    act.wait_ge(mix_in[a.b], 16 * (a.i + 1))
                    if even:
                        act.wait_ge(mix_set, a.t + 1)
                    act.wait_ge(summed, a.t + 1)
                    nc.scalar.copy(mix_high[a.b][:, :], mix[a.b]).then_inc(high_set, 1)

                def step(a):
                    b = a.b
                    p = a.plus(-1)
                    if p.exists(nt):
                        act.wait_ge(h_turned, p.t + 3)
                        if later(p):
                            act.wait_ge(routed, p.t)
                        nc.scalar.copy(hT, g.psum[:, 5:7, :].rearrange("p a n -> p (a n)")).then_inc(hT_set, 1)
                    q = a.plus(-2)
                    if q.exists(nt):
                        act.wait_ge(aff_turned, q.t + 1)
                        nc.scalar.copy(g.affT[:, bass.ds(P * q.t, P)], g.psum[0:NE, 7, P:2 * P]).then_inc(affT_set, 1)
                    if even and a.plus(1).exists(nt):
                        copy_r(a.plus(1))
                    if a.plus(1).exists(nt):
                        high(a.plus(1))
                    if a.exists(nt):
                        act.wait_ge(x_set, a.t + 1)
                        if later(a):
                            act.wait_ge(root, 2 * a.t - 1)
                        nc.scalar.activation(sq, x[b], ACT.Square, accum_out=ssq[:, :]).then_inc(squared, 1)
                    if p.exists(nt):
                        act.wait_ge(max_set, p.t + 1)
                        if later(p):
                            act.wait_ge(aff_set, p.t)
                        nc.scalar.activation(ex[:, :], g.psum[:, 7, 0:NE], ACT.Exp, bias=nmax[:, 0:1],
                                             accum_out=esum[:, :]).then_inc(exp_set, 1)
                if even:
                    copy_r(At(0, 0))
                high(At(0, 0))
                act.wait_ge(a_made, streams)
                run(act, step, nt // 2 + 1, 2, XT // 2 - 1)
                act.wait_ge(affT_set, nt)
        sem.release()


def load_piece(sp, io, g, expert, j):
    settle(sp, g)
    sp.dma_start(g.ring[:, j * PW:(j + 1) * PW], rows(io["moe_w"], expert * PIECES + j)).then_inc(g.piece_in[j], 16)


def routing(nc, io, g, layer):
    picks = [(0, SEQ, CAPX, 0)] + ([(SEQ, CTX, CAPC, CAPX)] if layer == 0 else [])
    with ExitStack() as st:
        tile = tiles_of(nc, st, f"ro{layer}")
        sem = Signals(nc, f"ro{layer}")
        val = tile("val", [NE, CAPX + CAPC])
        idx = tile("idx", [NE, CAPX + CAPC], U32)
        idf = tile("idf", [NE, CAPX + CAPC])
        found = [sem("found_x"), sem("found_c")]
        idf_set, turned, tabled = sem("idf_set"), sem("turned"), sem("tabled")
        mod = Modulation(nc, io, g, tile, sem, 1) if layer == 0 else None
        with nc.Block() as block:
            @block.sync
            def _(sp):
                if mod:
                    mod.sync(sp)
                for j in range(PREFETCH[layer]):
                    load_piece(sp, io, g, layer * NE, j)

            @block.vector
            def _(dve):
                if mod:
                    mod.vector()
                rounds = [cap // 8 for _, _, cap, _ in picks]
                for r in range(max(rounds)):
                    live = [(n, p) for n, p in enumerate(picks) if r < rounds[n]]
                    for turn in range(3):
                        for n, (a0, width, cap, v0) in live:
                            a = g.affT[:, a0:a0 + width]
                            v = val[:, v0 + 8 * r:v0 + 8 * r + 8]
                            if 3 * r + turn:
                                dve.wait_ge(found[n], 3 * r + turn)
                            if turn == 0:
                                last = nc.vector.max(v, a)
                            elif turn == 1:
                                last = nc.vector.max_index(idx[:, v0 + 8 * r:v0 + 8 * r + 8], v, a)
                            else:
                                last = nc.vector.match_replace(a, v, a, -1.0)
                            last.then_inc(found[n], 1)
                for n in range(len(picks)):
                    dve.wait_ge(found[n], 3 * rounds[n])
                wide = sum(p[2] for p in picks)
                nc.vector.tensor_copy(idf[:, 0:wide], idx[:, 0:wide]).then_inc(idf_set, 1)
                dve.wait_ge(turned, 1)
                nc.vector.tensor_copy(g.gate_x[:, :], g.psum[:, 0, NE:2 * NE]).then_inc(tabled, 1)
                nc.vector.tensor_copy(g.idx_x[:, :], g.psum[:, 0, 0:NE]).then_inc(tabled, 1)
                if layer == 0:
                    nc.vector.tensor_copy(g.gate_c[:, :], g.psum[0:CAPC, 1, NE:2 * NE]).then_inc(tabled, 1)
                    nc.vector.tensor_scalar(g.idx_c[:, :], g.psum[0:CAPC, 1, 0:NE], float(SEQ), None,
                                            ALU.add).then_inc(tabled, 1)

            @block.tensor
            def _(pe):
                if mod:
                    mod.tensor(pe)
                pe.wait_ge(idf_set, 1)
                one = g.ident[0:NE, 0:NE]
                for n, (_, _, cap, v0) in enumerate(picks):
                    nc.tensor.transpose(g.psum[0:cap, n, 0:NE], idf[:, v0:v0 + cap], one)
                    last = nc.tensor.transpose(g.psum[0:cap, n, NE:2 * NE], val[:, v0:v0 + cap], one)
                last.then_inc(turned, 1)

            @block.scalar
            def _(act):
                if mod:
                    mod.scalar(act)
        sem.release()


def experts(nc, io, g, layer):
    ctx_too = layer == 0
    n = CAPX + (CAPC if ctx_too else 0)
    per = BANK // n
    xbanks = -(-KD // per)
    acc = io["x1_d"] if layer == 0 else io["out"]
    base = 16 * NE * layer
    with ExitStack() as st:
        tile = tiles_of(nc, st, f"ex{layer}")
        sem = Signals(nc, f"ex{layer}")
        groups = [(CAPX, g.idx_x, g.gate_x)] + ([(CAPC, g.idx_c, g.gate_c)] if ctx_too else [])
        ng = len(groups)
        grow = [tile(f"grow{s}", [P, D]) for s in range(ng)]
        xs = [tile(f"xs{s}", [groups[s][0], D]) for s in range(ng)]
        accg = [tile(f"accg{s}", [groups[s][0], D]) for s in range(ng)]
        ys = [tile(f"ys{s}", [groups[s][0], D]) for s in range(ng)]
        xT = tile("xT", [P, KD, n])
        hT = tile("hT", [P, FB, n])
        yT = tile("yT", [P, KD, n])
        sil = [tile(f"sil{b}", [P, n]) for b in range(2)]
        row_in = sem("row_in")
        xs_in = [sem(f"xs_in{s}") for s in range(ng)]
        acc_in = [sem(f"acc_in{s}") for s in range(ng)]
        acc_out = [sem(f"acc_out{s}") for s in range(ng)]
        x_turned, xT_set = sem("x_turned"), sem("xT_set")
        gu, sil_set = sem("gu"), sem("sil_set")
        h_set = sem("h_set")
        down = sem("down")
        yT_set = sem("yT_set")
        y_turned = sem("y_turned")
        y_read = [sem(f"y_read{s}") for s in range(ng)]
        y_set = [sem(f"y_set{s}") for s in range(ng)]

        def slot(j):
            return g.ring[:, j * PW:(j + 1) * PW].rearrange("p (k n) -> p k n", k=KD)

        with nc.Block() as block:
            @block.sync
            def _(sp):
                for s in range(ng):
                    sp.dma_start(grow[s][:, :], mod_row(io["mod_d"], s, layer, G2)).then_inc(row_in, 16)
                for j in range(PREFETCH[layer], PIECES):
                    load_piece(sp, io, g, layer * NE, j)
                with sp.Fori(0, NE - 1) as e:
                    for j in range(4):
                        sp.wait_ge(gu, 8 * e + 2 * j + 2)
                        load_piece(sp, io, g, e + (layer * NE + 1), 2 * j)
                        load_piece(sp, io, g, e + (layer * NE + 1), 2 * j + 1)
                    for j in range(4):
                        sp.wait_ge(down, 8 * e + 2 * j + 2)
                        load_piece(sp, io, g, e + (layer * NE + 1), 8 + j)

            @block.gpsimd
            def _(pool):
                def gather(dst, src, idx, done):
                    pool.indirect_dma_start(dst[:, :], None, src, bass.IndirectOffsetOnAxis(ap=idx, axis=0)).then_inc(
                        done, 16)

                def tokens(e):
                    if e:
                        pool.wait_ge(x_turned, e)
                    for s, (cap, idx, _) in enumerate(groups):
                        gather(xs[s], io["h_d"], idx[:, e:e + 1], xs_in[s])
                tokens(0)
                for e in range(NE):
                    if e + 1 < NE:
                        tokens(e + 1)
                    for s, (cap, idx, _) in enumerate(groups):
                        if e:
                            pool.wait_ge(acc_out[s], 16 * e)
                        gather(accg[s], acc, idx[:, e:e + 1], acc_in[s])
                    for s, (cap, idx, _) in enumerate(groups):
                        pool.wait_ge(y_set[s], e + 1)
                        pool.indirect_dma_start(acc, bass.IndirectOffsetOnAxis(ap=idx[:, e:e + 1], axis=0),
                                                accg[s][:, :], None).then_inc(acc_out[s], 16)
                for s in range(ng):
                    pool.wait_ge(acc_out[s], 16 * NE)

            @block.tensor
            def _(pe):
                def turn_x(e, first=False):
                    for s in range(ng):
                        pe.wait_ge(xs_in[s], 16 * (e + 1))
                    if not first:
                        for s in range(ng):
                            if not (isinstance(e, int) and e < 2):
                                pe.wait_ge(y_read[s], e - 1)
                    for k in range(KD):
                        for s in range(ng):
                            cap, c0 = groups[s][0], (k % per) * n + (CAPX if s else 0)
                            last = nc.tensor.transpose(g.psum[:, k // per, c0:c0 + cap], xs[s][:, k * P:(k + 1) * P],
                                                       g.ident[0:cap, 0:cap])
                    last.then_inc(x_turned, 1)

                def turn_y(e):
                    pe.wait_ge(yT_set, 8 * e + 10)
                    for s in range(ng):
                        cap, c0 = groups[s][0], CAPX if s else 0
                        for k in range(KD):
                            bank = (k // 4) if s == 0 else (2 if k < 4 else 7)
                            last = nc.tensor.transpose(g.psum[0:cap, bank, (k % 4) * P:(k % 4 + 1) * P],
                                                       yT[:, k, c0:c0 + cap], g.ident[:, :])
                    last.then_inc(y_turned, 1)

                def step(e, first=False, final=False):
                    pe.wait_ge(xT_set, xbanks * (e + 1))
                    for f in range(FB):
                        j = f // 2
                        if f % 2 == 0:
                            for m in range(2):
                                pe.wait_ge(g.piece_in[2 * j + m], 16 * (e + 1) + base)
                        pe.wait_ge(h_set, 8 * e + f + 1)
                        for m in range(2):
                            for k in range(KD):
                                last = nc.tensor.matmul(g.psum[:, 3 + f % 2, m * n:(m + 1) * n],
                                                        slot(2 * j + m)[:, k, (f % 2) * P:(f % 2 + 1) * P], xT[:, k, :],
                                                        start=(k == 0), stop=(k == KD - 1))
                        last.then_inc(gu, 1)
                        if f == 0 and not first:
                            turn_y(e - 1)
                    if not final:
                        turn_x(e + 1)
                    pe.wait_ge(h_set, 8 * e + 10)
                    for k in range(KD):
                        if k % 2 == 0:
                            pe.wait_ge(g.piece_in[8 + k // 2], 16 * (e + 1) + base)
                        pe.wait_ge(yT_set, 8 * e + k + 1)
                        for f in range(FB):
                            last = nc.tensor.matmul(g.psum[:, 5 + k % 2, 0:n],
                                                    slot(8 + k // 2)[:, f, (k % 2) * P:(k % 2 + 1) * P], hT[:, f, :],
                                                    start=(f == 0), stop=(f == FB - 1))
                        last.then_inc(down, 1)
                turn_x(0, first=True)
                step(0, first=True)
                with pe.Fori(1, NE - 1) as e:
                    step(e)
                step(NE - 1, final=True)
                turn_y(NE - 1)

            @block.scalar
            def _(act):
                act.sem_inc(yT_set, 2)

                def copy_x(e):
                    act.wait_ge(x_turned, e + 1)
                    for bank in range(xbanks):
                        k0, k1 = bank * per, min(KD, (bank + 1) * per)
                        nc.scalar.copy(xT[:, k0:k1, :],
                                       g.psum[:, bank, 0:(k1 - k0) * n].rearrange("p (k n) -> p k n", n=n)).then_inc(
                            xT_set, 1)

                def step(e, final=False):
                    for f in range(FB):
                        act.wait_ge(gu, 8 * e + f + 1)
                        act.wait_ge(h_set, 8 * e + f + 1)
                        nc.scalar.activation(sil[f % 2][:, :], g.psum[:, 3 + f % 2, 0:n], ACT.Silu).then_inc(sil_set, 1)
                    if not final:
                        copy_x(e + 1)
                    for k in range(KD):
                        act.wait_ge(down, 8 * e + k + 1)
                        if k == 0 and not (isinstance(e, int) and e == 0):
                            act.wait_ge(y_turned, e)
                        nc.scalar.copy(yT[:, k, :], g.psum[:, 5 + k % 2, 0:n]).then_inc(yT_set, 1)
                copy_x(0)
                step(0)
                with act.Fori(1, NE - 1) as e:
                    step(e)
                step(NE - 1, final=True)

            @block.vector
            def _(dve):
                dve.sem_inc(h_set, 2)
                dve.wait_ge(row_in, 16 * ng)

                def rows_out(e, s):
                    cap, _, gate = groups[s]
                    dve.wait_ge(y_turned, e + 1)
                    banks = (0, 1) if s == 0 else (2, 7)
                    if not (isinstance(e, int) and e == 0):
                        dve.wait_ge(y_set[s], e)
                    for half in range(2):
                        c = slice(half * BANK, (half + 1) * BANK)
                        last = nc.vector.scalar_tensor_tensor(ys[s][:, c], g.psum[0:cap, banks[half], :],
                                                              gate[:, bass.ds(e, 1)], grow[s][0:cap, c],
                                                              ALU.mult, ALU.mult)
                    last.then_inc(y_read[s], 1)
                    dve.wait_ge(y_read[s], e + 1)
                    dve.wait_ge(acc_in[s], 16 * (e + 1))
                    nc.vector.tensor_tensor(accg[s][:, :], accg[s][:, :], ys[s][:, :], ALU.add).then_inc(y_set[s], 1)

                def step(e, first=False):
                    for f in range(FB):
                        dve.wait_ge(sil_set, 8 * e + f + 1)
                        if f == 0 and not first:
                            dve.wait_ge(down, 8 * e)
                        nc.vector.tensor_tensor(hT[:, f, :], sil[f % 2][:, :], g.psum[:, 3 + f % 2, n:2 * n],
                                                ALU.mult).then_inc(h_set, 1)
                        if f in (0, 2) and not first and f // 2 < ng:
                            rows_out(e - 1, f // 2)
                step(0, first=True)
                with dve.Fori(1, NE) as e:
                    step(e)
                for s in range(ng):
                    rows_out(NE - 1, s)
                    dve.wait_ge(y_set[s], NE)
        sem.release()


def latents(nc, io, g):
    w_in_n, w_uq_n, w_ukv_n = KD * (QL + KVL + ROPE), QL // P * AH * QKD, KVL // P * AH * 2 * NOPE
    with ExitStack() as st:
        tile = tiles_of(nc, st, "la")
        sem = Signals(nc, "la")
        carve = Carve(g.ring, w_in_n + w_uq_n + w_ukv_n)
        norm = Norm(nc, g, tile, sem)
        w_in = g.ring[:, 0:w_in_n].rearrange("p (k n) -> p k n", k=KD)
        w_uq = g.ring[:, w_in_n:w_in_n + w_uq_n].rearrange("p (k n) -> p k n", k=QL // P)
        w_ukv = g.ring[:, w_in_n + w_uq_n:w_in_n + w_uq_n + w_ukv_n].rearrange("p (k n) -> p k n", k=KVL // P)
        q = [carve(AH * QKD) for b in range(2)]
        kv = [carve(AH * 2 * NOPE) for b in range(2)]
        qnT, knT, qpT, kpT = (carve(AH * P) for n in range(4))
        qpT, kpT = qpT[0:ROPE, :], kpT[0:ROPE, :]
        hT = [tile(f"hT{b}", [P, D]) for b in range(2)]
        cs = [tile(f"cs{b}", [P, 2 * ROPE]) for b in range(2)]
        lat, cn, lsq = (tile(n, [P, QL + KVL]) for n in ("lat", "cn", "lsq"))
        pe_in = [tile(f"pe_in{b}", [P, ROPE]) for b in range(2)]
        cT = tile("cT", [P, QL + KVL])
        sqs = tile("sqs", [P, AH * QKD])
        qpr = [tile(f"qpr{b}", [P, AH * ROPE]) for b in range(2)]
        kpr = [tile(f"kpr{b}", [P, AH * ROPE]) for b in range(2)]
        qpg, tmp = tile("qpg", [P, AH * ROPE]), tile("tmp", [P, AH * ROPE])
        kpg, kp1 = tile("kpg", [P, ROPE]), tile("kp1", [P, ROPE])
        qa_row, kva_row = tile("qa_row", [P, QL]), tile("kva_row", [P, KVL])
        g_nope, g_rope = tile("g_nope", [P, 2]), tile("g_rope", [P, 2 * ROPE])
        lss, lms, lrs = (tile(n, [P, 2]) for n in ("lss", "lms", "lrs"))
        ss, hm, hr = (tile(n, [P, 2 * AH]) for n in ("ss", "hm", "hr"))
        pss, pq = tile("pss", [P, 1]), tile("pq", [P, ROPE])

        w_in_here, w_up_here, small_in, scaled_g = sem("w_in_here"), sem("w_up_here"), sem("small_in"), sem("scaled_g")
        cs_in = sem.pair("cs_in")
        hT_set = sem("hT_set")
        lat_sum = sem("lat_sum")
        lat_out = sem("lat_out")
        lat_sq, lat_root = sem("lat_sq"), sem("lat_root")
        cn_set = sem("cn_set")
        up = sem("up")
        up_out = sem("up_out")
        sums, hroot = sem("sums"), sem("hroot")
        roped = sem("roped")
        k_set = sem("k_set")
        turned = sem.pair("turned")
        t_out = sem.pair("t_out")
        v_out = sem.pair("v_out")
        heads_out = sem("heads_out")

        def in_all(a, latent, context):
            return latent * XT + context * (a.t - XT) if a.stream() else latent * a.t

        def ups(a):
            return in_all(a, 8, 4)

        def before_heads(a):
            return 5 * a.t + 2 if not (isinstance(a.i, int) and a.t > XT) else 5 * XT + 2 + 2 * (a.t - XT)

        def before_latent(a):
            return 0 if isinstance(a.i, int) and a.t == 0 else 5 * a.t - 4

        def later(a, n=0):
            return not (isinstance(a.i, int) and a.t <= n)

        with nc.Block() as block:
            @block.sync
            def _(sp):
                norm.load_rows(sp, io, 1, SC1, SH1, io["norm1_g"][1])
                for b in range(2):
                    norm.load(sp, At(0, b), io["x1_d"])
                    sp.sem_inc(v_out[b], 16)
                for dst, src in ((qa_row, io["q_a_g"].partition_broadcast(P)), (kva_row, io["kv_a_g"].partition_broadcast(P)),
                                 (g_nope, io["qk_g_nope"])):
                    sp.dma_start(dst[:, :], src).then_inc(small_in, 16)
                for m in range(2):
                    sp.dma_start(g_rope[:, m * ROPE:(m + 1) * ROPE], io["qk_g_rope"][m].partition_broadcast(P)).then_inc(
                        small_in, 16)
                sp.dma_start(g.ring[:, 0:w_in_n], io["od_w_in"]).then_inc(w_in_here, 16)
                sp.dma_start(g.ring[:, w_in_n:w_in_n + w_uq_n], io["w_uq"]).then_inc(w_up_here, 16)
                sp.dma_start(g.ring[:, w_in_n + w_uq_n:w_in_n + w_uq_n + w_ukv_n], io["w_ukv"]).then_inc(w_up_here, 16)

                def rope_rows(a):
                    if later(a, 1):
                        sp.wait_ge(k_set, 2 * (a.t - 1))
                    settle(sp, g)
                    sp.dma_start(cs[a.b][:, :], rows(io["rope_mla"], a.t)).then_inc(cs_in[a.b], 16)

                def store_v(a):
                    kvv = kv[a.b].rearrange("p (h m d) -> p h m d", h=AH, m=2)
                    sp.wait_ge(up_out, ups(a) + (6 if a.stream() else 10))
                    settle(sp, g)
                    sp.dma_start(rows(io["v_d"], a.t).rearrange("p (h d) -> p h d", h=AH), kvv[:, :, 1, :]).then_inc(
                        v_out[a.b], 16)

                def store_heads(a):
                    c = bass.ds(P * a.t, P)
                    for m in range(2):
                        sp.wait_ge(t_out[m], before_heads(a) + (3 if a.stream() else 5))
                    settle(sp, g)
                    jobs = [("kn_d", knT), ("kr_d", kpT)]
                    if not a.stream():
                        jobs += [("qn_d", qnT), ("qr_d", qpT)]
                    for name, src in jobs:
                        sp.dma_start(io[name].rearrange("p (h n) -> p h n", h=AH)[:, :, c],
                                     src.rearrange("p (h n) -> p h n", h=AH)).then_inc(heads_out, 16)

                def step(a):
                    if a.plus(2).exists(NT):
                        norm.load(sp, a.plus(2), io["x1_d"])
                    if a.plus(1).exists(NT):
                        rope_rows(a.plus(1))
                    if a.exists(NT):
                        store_v(a)
                    if a.plus(-1).exists(NT):
                        store_heads(a.plus(-1))
                rope_rows(At(0, 0))
                run(sp, step, NT // 2, 1, XT // 2 - 1)
                store_heads(At(NT // 2 - 1, 1))
                sp.wait_ge(heads_out, 16 * (4 * XT + 2 * CT))
                for b in range(2):
                    sp.wait_ge(v_out[b], 16 * (NT // 2 + 1))

            @block.tensor
            def _(pe):
                pe.sem_inc(norm.h_free, 2)
                pe.sem_inc(lat_sum, 2)

                def turn_h(a):
                    pe.wait_ge(norm.h_set, a.t + 1)
                    if later(a):
                        pe.wait_ge(hT_set, a.t)
                    transpose_tile(nc, g, 0, norm.h[a.b]).then_inc(norm.h_free, 1)

                def down(a):
                    pe.wait_ge(hT_set, a.t + 1)
                    if later(a):
                        pe.wait_ge(lat_out, a.t)
                    for bank, c0, width in ((2, 0, QL), (3, QL, KVL + ROPE)):
                        if bank == 2 and a.stream():
                            continue
                        for k in range(KD):
                            last = nc.tensor.matmul(g.psum[:, bank, 0:width], hT[a.b][:, k * P:(k + 1) * P],
                                                    w_in[:, k, c0:c0 + width], start=(k == 0), stop=(k == KD - 1))
                    last.then_inc(lat_sum, 1)

                def turn_latent(a):
                    n = before_latent(a)
                    pe.wait_ge(cn_set, a.t + 2)
                    for m in range(2):
                        pe.wait_ge(t_out[m], n + 1)
                        blocks = range(4) if m == 0 else range(4, 6)
                        transpose_tile(nc, g, 4 + m, cn, blocks).then_inc(turned[m], 1)

                def ups_of(a):
                    for m in range(2):
                        pe.wait_ge(t_out[m], before_latent(a) + 2)
                    n = ups(a)
                    chunks = [(w_uq, 0, QL // P, c * 384, 384) for c in range(4)] if not a.stream() else []
                    chunks += [(w_ukv, QL // P, KVL // P, c * BANK, BANK) for c in range(4)]
                    for m, (w, k0, nk, c0, width) in enumerate(chunks):
                        pe.wait_ge(up_out, n + m + 1)
                        for k in range(nk):
                            last = nc.tensor.matmul(g.psum[:, 6 + m % 2, 0:width], cT[:, (k0 + k) * P:(k0 + k + 1) * P],
                                                    w[:, k, c0:c0 + width], start=(k == 0), stop=(k == nk - 1))
                        last.then_inc(up, 1)

                def turn_heads(a):
                    n = before_heads(a)
                    pe.wait_ge(roped, in_all(a, 11, 5) + (6 if a.stream() else 12))
                    pe.wait_ge(k_set, 2 * (a.t + 1))
                    jobs = []
                    if not a.stream():
                        jobs += [(q[a.b], QKD, NOPE), (qpr[a.b], ROPE, ROPE)]
                    jobs += [(kv[a.b], 2 * NOPE, NOPE), (kpr[a.b], ROPE, ROPE)]
                    for j, (src, step_, width) in enumerate(jobs):
                        for m in range(2):
                            pe.wait_ge(t_out[m], n + j + 1)
                            settle(pe, g)
                            for h in range(4):
                                c0 = (4 * m + h) * step_
                                last = nc.tensor.transpose(g.psum[0:width, 4 + m, h * P:(h + 1) * P],
                                                           src[:, c0:c0 + width], g.ident[:, :])
                            last.then_inc(turned[m], 1)

                def step(a):
                    if a.plus(1).exists(NT):
                        turn_h(a.plus(1))
                    ups_of(a)
                    if a.plus(1).exists(NT):
                        down(a.plus(1))
                    if a.plus(-1).exists(NT):
                        turn_heads(a.plus(-1))
                    if a.plus(1).exists(NT):
                        turn_latent(a.plus(1))
                turn_h(At(0, 0))
                pe.wait_ge(w_in_here, 16)
                down(At(0, 0))
                turn_latent(At(0, 0))
                pe.wait_ge(w_up_here, 32)
                run(pe, step, NT // 2, 1, XT // 2 - 1)
                turn_heads(At(NT // 2 - 1, 1))

            @block.scalar
            def _(act):
                act.sem_inc(norm.squared, 1)
                act.sem_inc(up_out, 2)
                act.sem_inc(t_out[0], 1)
                act.sem_inc(t_out[1], 1)
                act.wait_ge(norm.a_made, 2)
                act.wait_ge(scaled_g, 1)

                def copy_h(a):
                    act.wait_ge(norm.h_free, a.t + 3)
                    act.wait_ge(lat_sum, a.t + 1)
                    nc.scalar.copy(hT[a.b][:, :], g.psum[:, 0:2, :].rearrange("p a n -> p (a n)")).then_inc(hT_set, 1)

                def copy_latent(a):
                    act.wait_ge(lat_sum, a.t + 3)
                    act.wait_ge(cn_set, a.t + 1)
                    if later(a, 1):
                        act.wait_ge(k_set, 2 * (a.t - 1))
                    if not a.stream():
                        nc.scalar.copy(lat[:, 0:QL], g.psum[:, 2, :])
                    nc.scalar.copy(pe_in[a.b][:, :], g.psum[:, 3, KVL:KVL + ROPE])
                    nc.scalar.copy(lat[:, QL:], g.psum[:, 3, 0:KVL]).then_inc(lat_out, 1)
                    act.wait_ge(lat_out, a.t + 1)
                    if later(a):
                        act.wait_ge(lat_sq, a.t)
                    if not a.stream():
                        nc.scalar.activation(lsq[:, 0:QL], lat[:, 0:QL], ACT.Square, accum_out=lss[:, 0:1])
                    nc.scalar.activation(lsq[:, QL:], lat[:, QL:], ACT.Square, accum_out=lss[:, 1:2]).then_inc(lat_sq, 1)

                def copy_turned_latent(a):
                    n = before_latent(a)
                    for m, (c0, c1) in enumerate(((0, QL), (QL, QL + KVL))):
                        act.wait_ge(turned[m], n + 1)
                        nc.scalar.copy(cT[:, c0:c1], g.psum[:, 4 + m, 0:c1 - c0]).then_inc(t_out[m], 1)

                def copy_ups(a):
                    n = ups(a)
                    qc = 0 if a.stream() else 4
                    act.wait_ge(v_out[a.b], 16 * (a.i + 1))
                    for m in range(qc + 4):
                        act.wait_ge(up, n + m + 1)
                        if m < qc:
                            dst, width = q[a.b][:, m * 384:(m + 1) * 384], 384
                        else:
                            dst, width = kv[a.b][:, (m - qc) * BANK:(m - qc + 1) * BANK], BANK
                        nc.scalar.copy(dst, g.psum[:, 6 + m % 2, 0:width]).then_inc(up_out, 1)

                def copy_heads(a):
                    n = before_heads(a)
                    if later(a):
                        act.wait_ge(heads_out, 64 * a.t if not (isinstance(a.i, int) and a.t > XT)
                                    else 64 * XT + 32 * (a.t - XT))
                    jobs = []
                    if not a.stream():
                        jobs += [(qnT, g_nope[:, 0:1], P), (qpT, None, ROPE)]
                    jobs += [(knT, g_nope[:, 1:2], P), (kpT, None, ROPE)]
                    for j, (dst, gain, height) in enumerate(jobs):
                        for m in range(2):
                            act.wait_ge(turned[m], n + j + 1)
                            src, out = g.psum[0:height, 4 + m, :], dst[:, m * BANK:(m + 1) * BANK]
                            if gain is None:
                                nc.scalar.copy(out, src).then_inc(t_out[m], 1)
                            else:
                                nc.scalar.activation(out, src, ACT.Identity, scale=gain).then_inc(t_out[m], 1)

                def step(a):
                    if a.plus(1).exists(NT):
                        copy_h(a.plus(1))
                    copy_ups(a)
                    if a.plus(2).exists(NT):
                        norm.square(act, a.plus(2))
                    if a.plus(1).exists(NT):
                        copy_latent(a.plus(1))
                    if a.plus(-1).exists(NT):
                        copy_heads(a.plus(-1))
                    if a.plus(1).exists(NT):
                        copy_turned_latent(a.plus(1))
                norm.square(act, At(0, 0))
                norm.square(act, At(0, 1))
                copy_h(At(0, 0))
                copy_latent(At(0, 0))
                copy_turned_latent(At(0, 0))
                run(act, step, NT // 2, 1, XT // 2 - 1)
                copy_heads(At(NT // 2 - 1, 1))

            @block.gpsimd
            def _(pool):
                pool.sem_inc(roped, 1)
                nc.gpsimd.memset(lss[:, :], 1.0).then_inc(lat_root, 1)
                pool.wait_ge(scaled_g, 1)

                def latent_root(a):
                    n = 3 * a.t + 1
                    pool.wait_ge(lat_sq, a.t + 1)
                    settle(pool, g)
                    nc.gpsimd.tensor_scalar(lms[:, 0:1], lss[:, 0:1], 1.0 / QL, EPS, ALU.mult, ALU.add).then_inc(lat_root, 1)
                    nc.gpsimd.tensor_scalar(lms[:, 1:2], lss[:, 1:2], 1.0 / KVL, EPS, ALU.mult, ALU.add).then_inc(lat_root, 1)
                    pool.wait_ge(lat_root, n + 2)
                    pool.wait_ge(cn_set, a.t + 1)
                    nc.gpsimd.tensor_tensor(lrs[:, :], lms[:, :], g.mhalf[:, 0:2], ALU.pow).then_inc(lat_root, 1)

                def heads(a):
                    b, s = a.b, a.stream()
                    n = in_all(a, 11, 5)
                    pool.wait_ge(sums, in_all(a, 7, 5) + (5 if s else 7))
                    if later(a):
                        pool.wait_ge(k_set, 2 * a.t)
                    settle(pool, g)
                    nc.gpsimd.tensor_scalar(hm[:, :], ss[:, :], 1.0 / QKD, EPS, ALU.mult, ALU.add).then_inc(hroot, 1)
                    pool.wait_ge(hroot, 2 * a.t + 1)
                    nc.gpsimd.tensor_tensor(hr[:, :], hm[:, :], g.mhalf[:, 0:2 * AH], ALU.pow).then_inc(hroot, 1)
                    pool.wait_ge(hroot, 2 * a.t + 2)
                    pool.wait_ge(cs_in[b], 16 * (a.i + 1))
                    pool.wait_ge(up_out, ups(a) + (6 if s else 10))
                    if later(a, 1):
                        pool.wait_ge(turned[1], 5 * a.t - 4)
                    if not s:
                        qv = heads_view(q[b], AH)
                        nc.gpsimd.tensor_tensor(qv, qv, per_head(hr[:, 0:AH], QKD, AH), ALU.mult).then_inc(roped, 1)
                        pool.wait_ge(roped, n + 2)
                        nc.gpsimd.tensor_tensor(heads_view(qpg[:, :], AH), qv[:, :, NOPE:],
                                                g_rope[:, 0:ROPE].unsqueeze(1).to_broadcast([P, AH, ROPE]),
                                                ALU.mult).then_inc(roped, 1)
                        rope_steps(nc, pool, roped, n + 2, heads_view(qpr[b][:, :], AH), heads_view(qpg[:, :], AH), cs[b],
                                   heads_view(tmp[:, :], AH), AH, ROPE // 4)
                        n += 6
                    nc.gpsimd.tensor_tensor(kpg[:, :], pe_in[b][:, :], g_rope[:, ROPE:], ALU.mult).then_inc(roped, 1)
                    rope_steps(nc, pool, roped, n + 1, heads_view(kp1[:, :], 1), heads_view(kpg[:, :], 1), cs[b],
                               heads_view(tmp[:, 0:ROPE], 1), 1, ROPE // 4)
                    n += 5
                    pool.wait_ge(roped, n + 1)
                    nc.gpsimd.tensor_tensor(heads_view(kpr[b][:, :], AH),
                                            kp1[:, :].unsqueeze(1).to_broadcast([P, AH, ROPE]),
                                            per_head(hr[:, AH:], ROPE, AH), ALU.mult).then_inc(k_set, 1)
                    kvv = kv[b].rearrange("p (h m d) -> p h m d", h=AH, m=2)[:, :, 0, :]
                    nc.gpsimd.tensor_tensor(kvv, kvv, per_head(hr[:, AH:], NOPE, AH), ALU.mult).then_inc(k_set, 1)

                def step(a):
                    if a.plus(2).exists(NT):
                        norm.root(pool, a.plus(2))
                    if a.plus(1).exists(NT):
                        latent_root(a.plus(1))
                    heads(a)
                norm.root(pool, At(0, 0))
                norm.root(pool, At(0, 1))
                latent_root(At(0, 0))
                run(pool, step, NT // 2, 1, XT // 2 - 1)

            @block.vector
            def _(dve):
                dve.sem_inc(norm.scaled, 2)
                dve.sem_inc(cn_set, 1)
                dve.wait_ge(small_in, 16 * 5)
                nc.vector.tensor_scalar(g_nope[:, 0:1], g_nope[:, 0:1], QKD ** -0.5, None, ALU.mult)
                nc.vector.tensor_scalar(g_rope[:, 0:ROPE], g_rope[:, 0:ROPE], QKD ** -0.5, None,
                                        ALU.mult).then_inc(scaled_g, 1)
                norm.make_a(dve)

                def latent_norm(a):
                    dve.wait_ge(lat_root, 3 * a.t + 4)
                    dve.wait_ge(lat_out, a.t + 1)
                    if later(a):
                        for m in range(2):
                            dve.wait_ge(turned[m], 1 if isinstance(a.i, int) and a.t == 1 else 5 * a.t - 8)
                    if not a.stream():
                        nc.vector.scalar_tensor_tensor(cn[:, 0:QL], lat[:, 0:QL], lrs[:, 0:1], qa_row[:, :],
                                                       ALU.mult, ALU.mult)
                    nc.vector.scalar_tensor_tensor(cn[:, QL:], lat[:, QL:], lrs[:, 1:2], kva_row[:, :],
                                                   ALU.mult, ALU.mult).then_inc(cn_set, 1)

                def head_sums(a):
                    b, s = a.b, a.stream()
                    n = in_all(a, 7, 5)
                    dve.wait_ge(up_out, ups(a) + (6 if s else 10))
                    if later(a):
                        dve.wait_ge(hroot, 2 * a.t - 1)
                    if not s:
                        nc.vector.tensor_tensor(sqs[:, :], q[b], q[b], ALU.mult).then_inc(sums, 1)
                        dve.wait_ge(sums, n + 1)
                        nc.vector.tensor_reduce(ss[:, 0:AH], heads_view(sqs[:, :], AH), AX.X, ALU.add).then_inc(sums, 1)
                        dve.wait_ge(sums, n + 2)
                        n += 2
                    kvv = kv[b].rearrange("p (h m d) -> p h m d", h=AH, m=2)[:, :, 0, :]
                    ksq = heads_view(sqs[:, 0:AH * NOPE], AH)
                    nc.vector.tensor_tensor(pq[:, :], pe_in[b][:, :], pe_in[b][:, :], ALU.mult).then_inc(sums, 1)
                    nc.vector.tensor_tensor(ksq, kvv, kvv, ALU.mult).then_inc(sums, 1)
                    dve.wait_ge(sums, n + 1)
                    nc.vector.tensor_reduce(pss[:, :], pq[:, :], AX.X, ALU.add).then_inc(sums, 1)
                    dve.wait_ge(sums, n + 2)
                    nc.vector.tensor_reduce(ss[:, AH:], ksq, AX.X, ALU.add).then_inc(sums, 1)
                    dve.wait_ge(sums, n + 4)
                    nc.vector.tensor_scalar(ss[:, AH:], ss[:, AH:], pss[:, 0:1], None, ALU.add).then_inc(sums, 1)
                    dve.wait_ge(sums, n + 5)

                def step(a):
                    head_sums(a)
                    if a.plus(2).exists(NT):
                        norm.scale(dve, a.plus(2))
                    if a.plus(1).exists(NT):
                        latent_norm(a.plus(1))
                norm.scale(dve, At(0, 0))
                norm.scale(dve, At(0, 1))
                latent_norm(At(0, 0))
                run(dve, step, NT // 2, 1, XT // 2 - 1)
        sem.release()


def attention(nc, io, g):
    per_head_units = XT
    body = 2 * per_head_units
    units = AH * per_head_units
    groups = ((0, 4), (4, 8), (8, 10))
    chunks = ((0, 512), (512, 1024), (1024, TOK))
    with ExitStack() as st:
        tile = tiles_of(nc, st, "at")
        sem = Signals(nc, "at")
        carve = Carve(g.ring, WOUT)
        raw_qn, raw_kn, raw_qp, raw_kp = (carve(w) for w in (SEQ, TOK, SEQ, TOK))
        qn, qn_low, qp = ([tile(f"{n}{s}", [P, SEQ], F32R) for s in range(2)] for n in ("qn", "qn_low", "qp"))
        kn, kn_low, kp, kp_low = ([tile(f"{n}{s}", [P, TOK], F32R) for s in range(2)]
                                  for n in ("kn", "kn_low", "kp", "kp_low"))
        v = [carve(KEYT * P).rearrange("p (k n) -> p k n", k=KEYT) for s in range(2)]
        prob = [carve(TOK) for b in range(2)]
        pT = carve(TOK)
        oT = [carve(SEQ) for s in range(2)]
        nmax, esum, inv = (tile(n, [P, 1]) for n in ("nmax", "esum", "inv"))
        v_in, o_out = sem.pair("v_in"), sem.pair("o_out")
        raw_in = sem("raw_in")
        high_set, low_set = sem("high_set"), sem("low_set")
        scored, max_set, exp_set, inv_set, normed = (sem(n) for n in ("scored", "max_set", "exp_set", "inv_set", "normed"))
        turned = sem("turned")
        copied_a, copied_v = sem("copied_a"), sem("copied_v")
        summed, o_set = sem("summed"), sem("o_set")

        def run_units(eng, slot):
            for u in range(body):
                slot(u, u, 0)
            with eng.Fori(1, units // body - 1) as i:
                for u in range(body):
                    slot(i * body + u, u, i)
            for n in range(units - body, units + 2):
                slot(n, n % body, n // body)

        def known(n):
            return isinstance(n, int)

        def split_part(u, i, first):
            s, part = u // per_head_units, u % per_head_units - first
            after = not (isinstance(i, int) and 2 * i + s + 1 >= AH)
            return (part, 1 - s, 8 * i + 4 * (s + 1) + part) if 0 <= part < 4 and after else None

        def high_part(act, part, s, count):
            act.wait_ge(raw_in, 96 if isinstance(count, int) and count < 4 else 24 * (count - part) + 96)
            src, dst = ((raw_qn, qn), (raw_kn, kn), (raw_qp, qp), (raw_kp, kp))[part]
            nc.scalar.copy(dst[s][:, :], src).then_inc(high_set, 1)

        def low_part(dve, part, s, count):
            dve.wait_ge(high_set, count + 1)
            lo = slice(ROPE, P) if part == 2 else slice(0, P)
            raw, high, low = ((raw_qn, qn, qn_low), (raw_kn, kn, kn_low), (raw_qp, qp, qp), (raw_kp, kp, kp_low))[part]
            nc.vector.tensor_tensor(low[s][lo, :], raw[lo, :], high[s][lo, :].bitcast(F32), ALU.subtract).then_inc(
                low_set, 1)

        with nc.Block() as block:
            @block.sync
            def _(sp):
                def load_raw(h):
                    for name, dst, width in (("qn_d", raw_qn, SEQ), ("kn_d", raw_kn, TOK),
                                             ("qr_d", raw_qp[0:ROPE, :], SEQ), ("qr_d", raw_qp[ROPE:P, :], SEQ),
                                             ("kr_d", raw_kp[0:ROPE, :], TOK), ("kr_d", raw_kp[ROPE:P, :], TOK)):
                        sp.dma_start(dst, io[name][:, bass.ds(h * width, width)]).then_inc(raw_in, 16)

                def load_v(i, s):
                    sp.dma_start(v[s], io["v_d"].rearrange("(t p) c -> p t c", p=P)[:, :, bass.ds((2 * i + s) * P, P)]
                                 ).then_inc(v_in[s], 16)

                def store(i, s):
                    sp.wait_ge(o_set, body * i + per_head_units * (s + 1))
                    settle(sp, g)
                    dst = io["mix_d"].rearrange("(t p) c -> p t c", p=P)[:, 0:XT, bass.ds((2 * i + s) * P, P)]
                    sp.dma_start(dst, oT[s].rearrange("p (t n) -> p t n", n=P)).then_inc(o_out[s], 16)
                load_raw(0)
                for s in range(2):
                    sp.sem_inc(o_out[s], 16)
                    load_v(0, s)
                sp.wait_ge(low_set, 4)
                load_raw(1)
                sp.dma_start(g.ring[:, 0:WOUT], io["od_w_out"]).then_inc(g.wout_in, 16)
                sp.dma_start(g.router[:, :], io["router_w"][1]).then_inc(g.wout_in, 16)
                with sp.Fori(0, AH // 2 - 1) as i:
                    for s in range(2):
                        sp.wait_ge(low_set, 8 * i + 4 * s + 8)
                        settle(sp, g)
                        load_raw(2 * i + (s + 2))
                        store(i, s)
                        sp.wait_ge(summed, body * i + per_head_units * (s + 1))
                        settle(sp, g)
                        load_v(i + 1, s)
                for s in range(2):
                    store(AH // 2 - 1, s)
                    sp.wait_ge(o_out[s], 16 * (AH // 2 + 1))

            @block.tensor
            def _(pe):
                def score(n, u, c):
                    s, t = u // per_head_units, u % per_head_units
                    k0, k1 = chunks[c]
                    o = g.psum[:, 3 * (u % 2) + c, 0:k1 - k0]
                    products = ((qn, kn), (qn, kn_low), (qn_low, kn), (qp, kp), (qp, kp_low))
                    for i, (q, k) in enumerate(products):
                        last = nc.tensor.matmul(o, q[s][:, t * P:(t + 1) * P], k[s][:, k0:k1],
                                                start=(i == 0), stop=(i == len(products) - 1))
                    return last

                def turn(m, u, j):
                    bank = 6 + j % 2
                    k0, k1 = groups[j]
                    for k in range(k0, k1):
                        last = nc.tensor.transpose(g.psum[:, bank, (k - k0) * P:(k - k0 + 1) * P],
                                                   prob[u % 2][:, k * P:(k + 1) * P], g.ident[:, :])
                    last.then_inc(turned, 1)

                def slot(n, u, i):
                    m, mu = n - 2, (u - 2) % body
                    back = not (known(n) and n < 2)
                    live = not (known(n) and n >= units)
                    if live and u % per_head_units == 0:
                        pe.wait_ge(low_set, 8 * i + 4 * (u // per_head_units) + 4)
                    if live and not (known(n) and n < 2):
                        pe.wait_ge(exp_set, n - 1)
                    for j in range(3):
                        if back:
                            if j == 0:
                                pe.wait_ge(normed, m + 1)
                                if not (known(m) and m == 0):
                                    pe.wait_ge(copied_v, 2 * m)
                            elif j == 1:
                                if not (known(m) and m == 0):
                                    pe.wait_ge(o_set, m)
                            else:
                                pe.wait_ge(copied_a, m + 1)
                            turn(m, mu, j)
                        if live:
                            last = score(n, u, j)
                            if j == 2:
                                last.then_inc(scored, 1)
                    if back:
                        pe.wait_ge(copied_v, 2 * m + 2)
                        if mu % per_head_units == 0:
                            pe.wait_ge(v_in[mu // per_head_units], 16 * i + 16)
                        for k in range(KEYT):
                            last = nc.tensor.matmul(g.psum[:, 7, 0:P], v[mu // per_head_units][:, k, :],
                                                    pT[:, k * P:(k + 1) * P], start=(k == 0), stop=(k == KEYT - 1))
                        last.then_inc(summed, 1)
                run_units(pe, slot)

            @block.vector
            def _(dve):
                def copy(m, j):
                    k0, k1 = groups[j]
                    dve.wait_ge(turned, 3 * m + j + 1)
                    if j == 1 and not (known(m) and m == 0):
                        dve.wait_ge(summed, m)
                    nc.vector.tensor_copy(pT[:, k0 * P:k1 * P], g.psum[:, 6 + j % 2, 0:(k1 - k0) * P]).then_inc(copied_v, 1)

                def slot(n, u, i):
                    p, pu = n - 1, (u - 1) % body
                    mid = not (known(n) and not 0 <= n - 1 < units)
                    back = not (known(n) and n < 2)
                    if mid:
                        b = pu % 2
                        dve.wait_ge(scored, p + 1)
                        s3 = g.psum[:, 3 * b:3 * b + 3, :].rearrange("p a n -> p (a n)")[:, 0:TOK]
                        if not (known(p) and p == 0):
                            dve.wait_ge(exp_set, p)
                        nc.vector.tensor_reduce(nmax[:, :], s3, AX.X, ALU.max, negate=True).then_inc(max_set, 1)
                        dve.wait_ge(exp_set, p + 1)
                        nc.vector.reciprocal(inv[:, :], esum[:, :]).then_inc(inv_set, 1)
                        dve.wait_ge(inv_set, p + 1)
                        nc.vector.tensor_scalar(prob[b], prob[b], inv[:, 0:1], None,
                                                ALU.mult).then_inc(normed, 1)
                        dve.wait_ge(normed, p + 1)
                    if back:
                        copy(n - 2, 1)
                        copy(n - 2, 2)
                    part = split_part(u, i, 2)
                    if part:
                        low_part(dve, *part)
                for part in range(4):
                    low_part(dve, part, 0, part)
                run_units(dve, slot)

            @block.scalar
            def _(act):
                def slot(n, u, i):
                    p, pu = n - 1, (u - 1) % body
                    m, mu = n - 2, (u - 2) % body
                    mid = not (known(n) and not 0 <= n - 1 < units)
                    back = not (known(n) and n < 2)
                    if mid:
                        b = pu % 2
                        act.wait_ge(max_set, p + 1)
                        if not (known(p) and p < 2):
                            act.wait_ge(turned, 3 * (p - 1))
                        if not (known(p) and p == 0):
                            act.wait_ge(inv_set, p)
                        s3 = g.psum[:, 3 * b:3 * b + 3, :].rearrange("p a n -> p (a n)")[:, 0:TOK]
                        nc.scalar.activation(prob[b], s3, ACT.Exp, bias=nmax[:, 0:1],
                                             accum_out=esum[:, :]).then_inc(exp_set, 1)
                    if back:
                        act.wait_ge(turned, 3 * m + 1)
                        if not (known(m) and m == 0):
                            act.wait_ge(summed, m)
                        k1 = groups[0][1] * P
                        nc.scalar.copy(pT[:, 0:k1], g.psum[:, 6, 0:k1]).then_inc(copied_a, 1)
                    part = split_part(u, i, 1)
                    if part:
                        high_part(act, *part)
                    if back:
                        act.wait_ge(summed, m + 1)
                        s, t = mu // per_head_units, mu % per_head_units
                        if t == 0:
                            act.wait_ge(o_out[s], 16 * (m // body + 1) if known(m) else m - mu + 16)
                        nc.scalar.copy(oT[s][:, t * P:(t + 1) * P], g.psum[:, 7, 0:P]).then_inc(o_set, 1)
                for part in range(4):
                    high_part(act, part, 0, part)
                run_units(act, slot)
        sem.release()


class Shared:

    def __init__(self, nc, st):
        def tile(name, shape, dt=F32):
            return st.enter_context(nc.sbuf_tensor(name, shape, dt))
        self.ring = tile("ring", [P, EVC * 2 * PW])
        self.ident = tile("ident", [P, P])
        self.mhalf = tile("mhalf", [P, 2 * AH])
        self.router = tile("router", [P, KD * NE])
        self.idx_x, self.idx_c = tile("idx_x", [CAPX, NE], U32), tile("idx_c", [CAPC, NE], U32)
        self.gate_x, self.gate_c = tile("gate_x", [CAPX, NE]), tile("gate_c", [CAPC, NE])
        self.psum = st.enter_context(nc.psum_tensor("psum", [P, 8, BANK], F32))
        self.ident_in, self.mhalf_set = nc.alloc_semaphore("ident_in"), nc.alloc_semaphore("mhalf_set")
        self.ev_conv_in, self.ev_ret_in = nc.alloc_semaphore("ev_conv_in"), nc.alloc_semaphore("ev_ret_in")
        self.tick = nc.alloc_semaphore("tick")
        self.wout_in = nc.alloc_semaphore("wout_in")
        self.wout_count = [32, 64]
        self.piece_in = [nc.alloc_semaphore(f"piece_in{j}") for j in range(PIECES)]


class Conv:
    def __init__(self, nc, st):
        self.u = st.enter_context(nc.sbuf_tensor("conv_u", [P, 4, UW], F32))
        self.y = st.enter_context(nc.sbuf_tensor("conv_y", [P, 4, TOK], F32))


def build(nc, io):
    with ExitStack() as st:
        g = Shared(nc, st)
        modulation(nc, io, g)
        with ExitStack() as inner:
            conv = Conv(nc, inner)
            conv_inputs(nc, io, g, conv)
            projections(nc, io, g, conv)
            retention(nc, io, g, conv)
        for layer in range(DEPTH):
            if layer == 1:
                latents(nc, io, g)
                attention(nc, io, g)
            with ExitStack() as inner:
                g.affT = inner.enter_context(nc.sbuf_tensor(f"affT{layer}", [NE, TOK], F32))
                mixer_out(nc, io, g, layer)
                routing(nc, io, g, layer)
            experts(nc, io, g, layer)


def lay_out(inputs, np):
    a = {k: np.asarray(v) for k, v in inputs.items()}

    def k_rows(w):
        k, n = w.shape
        return np.ascontiguousarray(w.reshape(k // P, P, n).transpose(1, 0, 2).reshape(P, -1))

    def chunks(w, width):
        k, n = w.shape
        return np.ascontiguousarray(
            w.reshape(k // P, P, n // width, width).transpose(2, 1, 0, 3).reshape(n // width * P, -1))

    pos = np.arange(SEQ)
    axis = [pos // 64, pos % 64]

    def rope(dim, pad):
        seg = dim // 4
        inv = np.float32(10000.0) ** (-(np.arange(seg, dtype=np.float32) / np.float32(seg)))
        ang = [p[:, None].astype(np.float32) * inv[None, :].astype(np.float32) for p in axis]
        c = np.concatenate([f for x in ang for f in (np.cos(x), np.cos(x))], axis=1)
        s = np.concatenate([f for x in ang for f in (-np.sin(x), np.sin(x))], axis=1)
        t = np.concatenate([c, s], axis=1)
        ctx = np.concatenate([np.ones((pad, dim)), np.zeros((pad, dim))], axis=1)
        return np.concatenate([t, ctx]).astype(np.float32)

    j, i = np.arange(P)[:, None], np.arange(P)[None, :]
    table = np.concatenate([np.maximum(i - j, 0), i >= j, np.maximum(j - i, 0), j >= i,
                            i + 1 + 0 * j, P - i + 0 * j, P - 1 - j, j], axis=1).astype(np.float32)
    ev = a["ev_w_in"][0]
    ev = np.concatenate([ev[:, 5 * HALF:], ev[:, :5 * HALF]], axis=1)
    gu = np.stack([a["moe_w_gate"], a["moe_w_up"]], axis=2)
    gu = gu.reshape(DEPTH * NE, 2, KD, P, 4, 256).transpose(0, 4, 1, 3, 2, 5).reshape(DEPTH * NE, 8, P, PW)
    dn = a["moe_w_down"].reshape(DEPTH * NE, FB, P, 4, 256).transpose(0, 3, 2, 1, 4).reshape(DEPTH * NE, 4, P, PW)
    qk = np.stack([a["mla_qk_g_q"][0], a["mla_qk_g_k"][0]])
    return {
        "tok": np.concatenate([a["x"][0], a["ctx"][0]]),
        "cc": np.stack([a["c"][0].reshape(KD, P), a["c_ctx"].reshape(KD, P)], axis=-1).transpose(1, 0, 2).reshape(P, -1),
        "ident_d": np.eye(P, dtype=np.float32),
        "mod_w": np.concatenate([chunks(w, BANK) for w in a["mod_w"]]),
        "mod_b": a["mod_b"].reshape(-1, BANK),
        "norm1_g": a["norm1_g"], "norm2_g": a["norm2_g"],
        "ev_w_in": chunks(ev, HALF),
        "ret_gn_g": a["ret_gn_g"][0],
        "ret_logit": np.concatenate([a["ret_decay_f"][0], a["ret_decay_b"][0]]),
        "ret_table": table,
        "rope_ret": rope(HD, CTX), "rope_mla": rope(ROPE, CTX),
        "conv_w": a["conv_w"][0].reshape(TAPS, 4, P).transpose(2, 1, 0).reshape(P, -1),
        "conv_b": a["conv_b"][0].reshape(4, P).T,
        "conv_ln": np.concatenate([a["conv_ln_g"][0].reshape(4, P), a["conv_ln_b"][0].reshape(4, P)]).T,
        "ev_w_out": k_rows(a["ev_w_out"][0]), "od_w_out": k_rows(a["od_w_out"][0]),
        "router_w": np.stack([k_rows(w) for w in a["router_w"]]),
        "moe_w": np.concatenate([gu, dn], axis=1).reshape(-1, PW),
        "od_w_in": k_rows(a["od_w_in"][0]),
        "q_a_g": a["mla_q_a_g"][0], "kv_a_g": a["mla_kv_a_g"][0],
        "w_uq": k_rows(a["mla_w_uq"][0]), "w_ukv": k_rows(a["mla_w_ukv"][0]),
        "qk_g_nope": qk[:, :NOPE].T, "qk_g_rope": qk[:, NOPE:],
    }


_SCRATCH = {"mod_d": (2, DEPTH * NMOD), "hT_d": (TOK, D), "rec_d": ((NT + 2) * P, RECW), "ret_f_d": ((NT + 2) * P, HALF),
            "ret_b_d": ((NT + 2) * P, HALF), "mix_d": (TOK, D), "x1_d": (TOK, D), "h_d": (TOK, D),
            "qn_d": (P, AH * SEQ), "qr_d": (ROPE, AH * SEQ), "kn_d": (P, AH * TOK), "kr_d": (ROPE, AH * TOK),
            "v_d": (TOK, D)}


def kernel(**inputs):
    import numpy as np
    import concourse.bacc as bacc
    from concourse.bass_utils import run_bass_kernel_spmd

    nc = bacc.Bacc("TRN2", target_bir_lowering=False, num_devices=1)
    arrays, io = {}, {}
    for name, value in lay_out(inputs, np).items():
        arrays["in_" + name] = np.ascontiguousarray(value)
        io[name] = nc.dram_tensor("in_" + name, value.shape, F32, kind="ExternalInput").ap()
    for name, shape in _SCRATCH.items():
        io[name] = nc.dram_tensor(name, shape, F32, kind="Internal").ap()
    io["ret_d"] = (io["ret_f_d"], io["ret_b_d"])
    io["out"] = nc.dram_tensor("out_x", (SEQ, D), F32, kind="ExternalOutput").ap()
    build(nc, io)
    got = run_bass_kernel_spmd(nc, [arrays], core_ids=[0]).results[0]
    return got["out_x"].reshape(1, SEQ, D)
```
